# Optimizing a Trainium2 kernel written in Bass

```python
import jax, jax.numpy as jnp
from jax import lax
import numpy as np

D_MODEL = 2048
BATCH = 1
SEQ = 256
DEPTH = 1

N_HEADS_DIFF = 8
DIFF_HEAD_DIM = 64
DIFF_V_DIM = 2 * DIFF_HEAD_DIM
DIFF_QK_WIDTH = N_HEADS_DIFF * 2 * DIFF_HEAD_DIM
DIFF_WIDTH = N_HEADS_DIFF * DIFF_V_DIM
N_HEADS_SB = 8
SB_HEAD_DIM = 128
SB_WIDTH = N_HEADS_SB * SB_HEAD_DIM
IN_PROJ_WIDTH = 2 * DIFF_QK_WIDTH + DIFF_WIDTH + 3 * SB_WIDTH
SPLIT_POINTS = (DIFF_QK_WIDTH, 2 * DIFF_QK_WIDTH, 2 * DIFF_QK_WIDTH + DIFF_WIDTH,
                2 * DIFF_QK_WIDTH + DIFF_WIDTH + SB_WIDTH,
                2 * DIFF_QK_WIDTH + DIFF_WIDTH + 2 * SB_WIDTH)
N_BRANCHES = 2
ROT_DIM = DIFF_HEAD_DIM // 4
ROPE_THETA = 500000.0
Q_BLOCK = 128
N_GROUPS = 4
EXPERTS_PER_GROUP = 8
N_EXPERTS = N_GROUPS * EXPERTS_PER_GROUP
TOP_K_IN_GROUP = 2
EXPERT_FF = D_MODEL // 4
EPS = 1e-6
NEG_INF = float(np.finfo(np.float32).min)

kernel_name = "hybrid_diffattn_stickbreak_hmoe"

def rms_norm(x, g):
    xf = x.astype(jnp.float32)
    y = xf * lax.rsqrt(jnp.mean(xf * xf, axis=-1, keepdims=True) + EPS)
    return (y * g.astype(jnp.float32)).astype(x.dtype)

def partial_rope(t, cos, sin):
    half = ROT_DIM // 2
    t1 = t[..., :half]
    t2 = t[..., half:ROT_DIM]
    return jnp.concatenate([t1 * cos - t2 * sin, t2 * cos + t1 * sin, t[..., ROT_DIM:]], axis=-1)

def diff_attention(q1, q2, k1, k2, v, lam):
    s_len = q1.shape[2]
    scale = DIFF_HEAD_DIM ** -0.5
    kpos = jnp.arange(s_len)

    def block(i):
        start = i * Q_BLOCK
        qpos = start + jnp.arange(Q_BLOCK)
        mask = kpos[None, :] <= qpos[:, None]

        def probs(q, k):
            qb = lax.dynamic_slice_in_dim(q, start, Q_BLOCK, axis=2)
            s = jnp.einsum('bhqd,bhkd->bhqk', qb, k) * scale
            return jax.nn.softmax(jnp.where(mask, s, NEG_INF), axis=-1)

        a = probs(q1, k1) - lam * probs(q2, k2)
        return jnp.einsum('bhqk,bhkd->bhqd', a, v)

    return lax.map(block, jnp.arange(s_len // Q_BLOCK))

def stick_breaking_attention(q, k, v):
    s_len = q.shape[2]
    scale = SB_HEAD_DIM ** -0.5
    kpos = jnp.arange(s_len)

    def block(i):
        start = i * Q_BLOCK
        qpos = start + jnp.arange(Q_BLOCK)
        mask = kpos[None, :] < qpos[:, None]
        qb = lax.dynamic_slice_in_dim(q, start, Q_BLOCK, axis=2)
        z = jnp.einsum('bhqd,bhkd->bhqk', qb, k) * scale
        log_beta = jax.nn.log_sigmoid(z)
        log_one_minus = jnp.where(mask, jax.nn.log_sigmoid(-z), 0.0)
        suffix = lax.cumsum(log_one_minus, axis=3, reverse=True) - log_one_minus
        a = jnp.where(mask, jnp.exp(log_beta + suffix), 0.0)
        return jnp.einsum('bhqk,bhkd->bhqd', a, v)

    return lax.map(block, jnp.arange(s_len // Q_BLOCK))

def merge_blocks(o):
    nb, b, h, blk, d = o.shape
    return o.transpose(1, 0, 3, 2, 4).reshape(b, nb * blk, h, d)

def setup_inputs(seed: int = 0) -> dict:
    key = jax.random.key(seed)
    ks = jax.random.split(key, 20)
    f32 = jnp.float32
    nrm = lambda k, shape, s: jax.random.normal(k, shape, f32) * s
    x = jax.random.normal(ks[0], (BATCH, SEQ, D_MODEL), f32)
    offsets = jax.random.randint(ks[1], (BATCH, 1), 0, 4096, dtype=jnp.int32)
    positions = offsets + jnp.arange(SEQ, dtype=jnp.int32)[None, :]
    return {
        "x": x,
        "positions": positions,
        "g_mix": 1.0 + nrm(ks[2], (DEPTH, D_MODEL), 0.01),
        "w_in": nrm(ks[3], (DEPTH, D_MODEL, IN_PROJ_WIDTH), D_MODEL ** -0.5),
        "w_gate": nrm(ks[4], (DEPTH, D_MODEL, N_BRANCHES * D_MODEL), D_MODEL ** -0.5),
        "lambda_params": nrm(ks[5], (DEPTH, 4, DIFF_HEAD_DIM), 0.1),
        "g_subln": 1.0 + nrm(ks[6], (DEPTH, DIFF_V_DIM), 0.01),
        "w_br_diff": nrm(ks[7], (DEPTH, DIFF_WIDTH, D_MODEL), DIFF_WIDTH ** -0.5),
        "w_br_sb": nrm(ks[8], (DEPTH, SB_WIDTH, D_MODEL), SB_WIDTH ** -0.5),
        "w_out": nrm(ks[9], (DEPTH, D_MODEL, D_MODEL), D_MODEL ** -0.5),
        "g_moe": 1.0 + nrm(ks[10], (DEPTH, D_MODEL), 0.01),
        "w_group": nrm(ks[11], (DEPTH, D_MODEL, N_GROUPS), D_MODEL ** -0.5),
        "b_group": nrm(ks[12], (DEPTH, N_GROUPS), 0.01),
        "w_router": nrm(ks[13], (DEPTH, D_MODEL, N_EXPERTS), D_MODEL ** -0.5),
        "b_router": nrm(ks[14], (DEPTH, N_EXPERTS), 0.01),
        "w_up_gate": nrm(ks[15], (DEPTH, N_EXPERTS, D_MODEL, EXPERT_FF), D_MODEL ** -0.5),
        "w_up": nrm(ks[16], (DEPTH, N_EXPERTS, D_MODEL, EXPERT_FF), D_MODEL ** -0.5),
        "w_down": nrm(ks[17], (DEPTH, N_EXPERTS, EXPERT_FF, D_MODEL), EXPERT_FF ** -0.5),
        "g_final": 1.0 + nrm(ks[18], (D_MODEL,), 0.01),
    }

def reference(x, positions, g_mix, w_in, w_gate, lambda_params, g_subln, w_br_diff, w_br_sb,
              w_out, g_moe, w_group, b_group, w_router, b_router, w_up_gate, w_up, w_down,
              g_final):
    f32 = jnp.float32
    b, s, d = x.shape
    t_tok = b * s
    inv_freq = ROPE_THETA ** (-jnp.arange(0, ROT_DIM, 2, dtype=f32) / ROT_DIM)
    ang = positions.astype(f32)[..., None] * inv_freq
    cos = jnp.cos(ang)[:, :, None, None, :]
    sin = jnp.sin(ang)[:, :, None, None, :]

    for l in range(DEPTH):
        h = rms_norm(x, g_mix[l])
        proj = h @ w_in[l]
        dq, dk, dv, sq, sk, sv = jnp.split(proj, SPLIT_POINTS, axis=-1)

        dq = partial_rope(dq.astype(f32).reshape(b, s, N_HEADS_DIFF, 2, DIFF_HEAD_DIM), cos, sin)
        dk = partial_rope(dk.astype(f32).reshape(b, s, N_HEADS_DIFF, 2, DIFF_HEAD_DIM), cos, sin)
        dq = dq.transpose(0, 2, 3, 1, 4)
        dk = dk.transpose(0, 2, 3, 1, 4)
        dv = dv.astype(f32).reshape(b, s, N_HEADS_DIFF, DIFF_V_DIM).transpose(0, 2, 1, 3)
        lp = lambda_params[l].astype(f32)
        lambda_init = 0.8 - 0.6 * np.exp(-0.3 * l)
        lam = jnp.exp(jnp.sum(lp[0] * lp[1])) - jnp.exp(jnp.sum(lp[2] * lp[3])) + lambda_init
        o_diff = merge_blocks(diff_attention(dq[:, :, 0], dq[:, :, 1], dk[:, :, 0], dk[:, :, 1], dv, lam))
        o_diff = rms_norm(o_diff, g_subln[l]) * (1.0 - lambda_init)
        y_diff = o_diff.reshape(b, s, DIFF_WIDTH).astype(x.dtype) @ w_br_diff[l]

        sq = sq.astype(f32).reshape(b, s, N_HEADS_SB, SB_HEAD_DIM).transpose(0, 2, 1, 3)
        sk = sk.astype(f32).reshape(b, s, N_HEADS_SB, SB_HEAD_DIM).transpose(0, 2, 1, 3)
        sv = sv.astype(f32).reshape(b, s, N_HEADS_SB, SB_HEAD_DIM).transpose(0, 2, 1, 3)
        o_sb = merge_blocks(stick_breaking_attention(sq, sk, sv))
        y_sb = o_sb.reshape(b, s, SB_WIDTH).astype(x.dtype) @ w_br_sb[l]

        gates = jax.nn.sigmoid((h @ w_gate[l]).astype(f32)).reshape(b, s, N_BRANCHES, d)
        mixed = (gates[:, :, 0] * y_diff.astype(f32) + gates[:, :, 1] * y_sb.astype(f32)).astype(x.dtype)
        x = x + mixed @ w_out[l]

        hn = rms_norm(x, g_moe[l]).reshape(t_tok, d)
        group_probs = jax.nn.softmax((hn @ w_group[l]).astype(f32) + b_group[l].astype(f32), axis=-1)
        g_val, g_idx = lax.top_k(group_probs, 1)
        e_logits = ((hn @ w_router[l]).astype(f32) + b_router[l].astype(f32)).reshape(
            t_tok, N_GROUPS, EXPERTS_PER_GROUP)
        e_sel = jnp.take_along_axis(e_logits, g_idx[:, :, None], axis=1)[:, 0]
        e_val, e_idx = lax.top_k(e_sel, TOP_K_IN_GROUP)
        e_w = jax.nn.softmax(e_val, axis=-1) * g_val
        flat_idx = g_idx * EXPERTS_PER_GROUP + e_idx
        combine = jnp.sum(jax.nn.one_hot(flat_idx, N_EXPERTS, dtype=f32) * e_w[..., None], axis=1)
        acc = jnp.zeros((t_tok, d), f32)
        for e in range(N_EXPERTS):
            y_e = (jax.nn.silu(hn @ w_up_gate[l, e]) * (hn @ w_up[l, e])) @ w_down[l, e]
            acc = acc + combine[:, e:e + 1] * y_e.astype(f32)
        x = x + acc.reshape(b, s, d).astype(x.dtype)

    return rms_norm(x, g_final)


_drawn_inputs = setup_inputs


def setup_inputs(seed=0):
    import zlib

    import numpy as np

    out = dict(_drawn_inputs(seed))
    spreads = {}
    factors = {'g_mix': 2.852,
     'g_subln': 3.942,
     'g_moe': 10.064,
     'b_group': 3.396,
     'b_router': 27.991,
     'g_final': 184.116}
    for name, (base, spread) in spreads.items():
        noise = np.random.default_rng([zlib.crc32(name.encode()), seed]).standard_normal(out[name].shape)
        drawn = base * np.exp(spread * noise) if base else spread * noise
        out[name] = __import__('jax').numpy.asarray(drawn.astype(out[name].dtype))
    for name, factor in factors.items():
        out[name] = (out[name] * factor).astype(out[name].dtype)
    return out
```

```python
from contextlib import ExitStack

import numpy as np

import concourse.bass as bass
from concourse import mybir
from concourse.alu_op_type import AluOpType as ALU

F32 = mybir.dt.float32
I32 = mybir.dt.int32
ACT = mybir.ActivationFunctionType
AX = mybir.AxisListType.X

P = 128
BLK = 512
ROPE_THETA = 500000.0
EPS = 1e-6
LAMBDA_INIT = 0.8 - 0.6 * float(np.exp(-0.3 * 0))
BIG = 1e30
RING = 4
SLOTS = 32
SIDE = 4
TWO_PI = (6.28125, 0.0019350051879882812, 3.0199159819e-07)
ROUND = float(3 << 22)
TYPES = 6
DQ, DK, DV, SQ, SK, SV = range(TYPES)


def decoder_block(nc, x, positions, g_mix, w_in, w_gate, lambda_params, g_subln, w_br_diff,
                  w_br_sb, w_out, g_moe, w_group, b_group, w_router, b_router, w_up_gate, w_up,
                  w_down, g_final, out):
    _, T, D = x.shape
    TT = T // P
    KD = D // P
    HV = g_subln.shape[1]
    HQ = lambda_params.shape[2]
    HEADS = w_br_diff.shape[1] // HV
    HALF = HQ // 4 // 2
    NG = w_group.shape[2]
    NE = w_router.shape[2]
    PER = NE // NG
    FF = w_up.shape[3]
    IN_BLOCKS = w_in.shape[2] // BLK
    GATE_BLOCKS = w_gate.shape[2] // BLK
    OUT_BLOCKS = D // BLK
    assert TT == 2 and HV == P and 2 * HQ == P and w_in.shape[2] == TYPES * HEADS * P
    assert GATE_BLOCKS == HEADS and FF == BLK and OUT_BLOCKS == 4 and KD == 16
    KH = KD // 2
    PAIR = 2
    GROUPS = NE // SIDE
    MAX_PASSES = T // SLOTS
    TURN_GATE = IN_BLOCKS // PAIR
    TURN_BR = TURN_GATE + GATE_BLOCKS // PAIR
    TURN_OUT = TURN_BR + 2 * OUT_BLOCKS // RING
    TURN_MOE = TURN_OUT + 2 * OUT_BLOCKS // RING
    MOE_TURNS = (KD + 2 * (FF // P)) // RING
    USED_MOE = RING * TURN_MOE

    ctx = ExitStack()
    with ctx:
        def sb(name, shape, dt=F32):
            return ctx.enter_context(nc.sbuf_tensor(name, shape, dt))

        def sem(name):
            return ctx.enter_context(nc.semaphore(name))

        ring = sb("ring", [P, RING, KH * BLK])
        x_tok = sb("x_tok", [P, TT, D])
        hT = sb("hT", [P, KD, T])
        qkv = sb("qkv", [P, TT, TYPES, HEADS, P])
        gates = sb("gates", [P, TT, 2 * D])
        qkv_flat = qkv[:, :, :, :, :].rearrange("p a b c d -> p (a b c d)")

        def part(flat, at, *shape):
            n = int(np.prod(shape))
            v = flat[:, at:at + n]
            if len(shape) == 2:
                return v.rearrange("p (a b) -> p a b", a=shape[0])
            if len(shape) == 3:
                return v.rearrange("p (a b c) -> p a b c", a=shape[0], b=shape[1])
            return v

        mixT = part(qkv_flat, 0, KD, T)
        xgT = part(qkv_flat, 4096, KD, P)
        y_sb = part(qkv_flat, 6144, D)
        act_sb = part(qkv_flat, 8192, 2, BLK)
        actT = part(qkv_flat, 9216, FF // P, P)
        pick = part(qkv_flat, 9728, 2, TT, P)
        placeT = part(qkv_flat, 10240, T)
        routing = part(qkv_flat, 10496, 1792)
        gates_flat = gates[:, :, :].rearrange("p a b -> p (a b)")
        normed = part(gates_flat, 0, TT, D)
        g_final_sb = part(gates_flat, 4096, D)
        junk = part(gates_flat, 6144, D)
        rope_tmp = part(gates_flat, 0, 4, 2 * 2 * HEADS, HALF)

        at = [0]

        def small(*shape):
            v = part(routing, at[0], *shape)
            at[0] += int(np.prod(shape))
            return v

        logits = small(TT, NG + NE)
        best = small(TT, 4)
        shifted = small(TT, NG + 1)
        is_group = small(TT, NG)
        masked = small(TT, NE)
        is_top = [small(TT, NE), small(TT, NE)]
        tie = small(TT, NE)
        tie_top = small(TT, 1)
        chosen = small(TT, NE)
        combine = small(TT, NE)
        rank = small(TT, NE)
        pair_w = small(TT, 4)
        over = small(MAX_PASSES - 1)
        count = small(2)

        stage = sb("stage", [P, TT, 4, P])
        qkT = sb("qkT", [P, 4, T])
        prob = sb("prob", [P, 2, 3 * P])
        diff = sb("diff", [P, 3 * P])
        z = sb("z", [P, 3 * P])
        soft = sb("soft", [P, 3 * P])
        stick = sb("stick", [P, 3 * P])
        aT_diff = sb("aT_diff", [P, 3 * P])
        aT_sb = sb("aT_sb", [P, 3 * P])
        ident = sb("ident", [P, P])
        before = sb("before", [P, P])
        ones = sb("ones", [P, P])
        mask_upto = sb("mask_upto", [P, 3 * P])
        mask_before = sb("mask_before", [P, 3 * P])
        gsub = sb("gsub", [P, HV])
        slot_id = sb("slot_id", [P, SLOTS])
        falling = sb("falling", [P, NE])
        starts = sb("starts", [P, MAX_PASSES - 1])
        inv_freq = sb("inv_freq", [P, HALF])
        g_mix_sb = sb("g_mix_sb", [P, KD])
        g_moe_sb = sb("g_moe_sb", [P, KD])
        w_route = sb("w_route", [P, KD, NG + NE])
        b_route = sb("b_route", [P, NG + NE])
        lam_sb = sb("lam_sb", [P, 4, HQ])
        pos_i = sb("pos_i", [P, TT], I32)
        passes_i = sb("passes_i", [P, 1], I32)
        pos_f = sb("pos_f", [P, TT])
        angle = sb("angle", [P, TT, HALF])
        whole = sb("whole", [P, TT, HALF])
        sin = sb("sin", [P, TT, HALF])
        cos = sb("cos", [P, TT, HALF])
        lam_two = sb("lam_two", [P, 2])
        neg_lam = sb("neg_lam", [P, 1])
        top = sb("top", [P, TT, 2])
        neg_top = sb("neg_top", [P, TT, 2])
        total = sb("total", [P, TT, 2])
        weight = sb("weight", [P, TT, 2])
        ssq = sb("ssq", [P, TT, OUT_BLOCKS])
        var = sb("var", [P, TT])
        rstd = sb("rstd", [P, TT])
        newton = sb("newton", [P, TT])

        bank = [ctx.enter_context(nc.psum_tensor(f"bank{i}", [P, BLK], F32)) for i in range(8)]

        x_in = sem("x_in")
        consts_in = sem("consts_in")
        g_final_in = sem("g_final_in")
        out_written = sem("out_written")
        slot_full = [sem(f"slot_full{i}") for i in range(RING)]
        slots_used = sem("slots_used")
        masks_made = sem("masks_made")
        rope_made = sem("rope_made")
        sines_made = sem("sines_made")
        angles_made = sem("angles_made")
        lam_summed = sem("lam_summed")
        lam_exped = sem("lam_exped")
        squared = sem("squared")
        var_made = sem("var_made")
        rstd_guess = sem("rstd_guess")
        rstd_made = sem("rstd_made")
        normed_act = sem("normed_act")
        normed_dve = sem("normed_dve")
        turned = sem("turned")
        turned_act = sem("turned_act")
        turned_dve = sem("turned_dve")
        proj_act = sem("proj_act")
        proj_dve = sem("proj_dve")
        staged = sem("staged")
        qk_turned = sem("qk_turned")
        qkT_act = sem("qkT_act")
        qkT_dve = sem("qkT_dve")
        diff_scored = sem("diff_scored")
        sb_scored = sem("sb_scored")
        tops_made = sem("tops_made")
        z_made = sem("z_made")
        diff_exped = sem("diff_exped")
        soft_made = sem("soft_made")
        stick_summed = sem("stick_summed")
        stick_exped = sem("stick_exped")
        diff_made = sem("diff_made")
        diff_turned = sem("diff_turned")
        sb_turned = sem("sb_turned")
        aT_act = sem("aT_act")
        aT_dve = sem("aT_dve")
        heads_out = sem("heads_out")
        head_squared = sem("head_squared")
        head_var = sem("head_var")
        head_guess = sem("head_guess")
        heads_stored = sem("heads_stored")
        gates_open = sem("gates_open")
        mixed = sem("mixed")
        mix_turned = sem("mix_turned")
        mixT_made = sem("mixT_made")
        x_added = sem("x_added")
        logits_made = sem("logits_made")
        route_shifted = sem("route_shifted")
        route_exped = sem("route_exped")
        chosen_made = sem("chosen_made")
        ranks_made = sem("ranks_made")
        passes_made = sem("passes_made")
        picks_made = sem("picks_made")
        gathered = sem("gathered")
        xg_made = sem("xg_made")
        place_turned = sem("place_turned")
        placeT_made = sem("placeT_made")
        silu_made = sem("silu_made")
        act_made = sem("act_made")
        act_turned = sem("act_turned")
        actT_made = sem("actT_made")
        y_act = sem("y_act")
        y_dve = sem("y_dve")
        combined = sem("combined")
        added = sem("added")
        x_final = sem("x_final")
        out_made = sem("out_made")

        x_d = x[0].rearrange("(t p) d -> t p d", p=P)
        out_d = out[0].rearrange("(t p) d -> t p d", p=P)
        w_in_d = w_in[0].rearrange("(h q k p) (b n) -> h q b p k n", h=2, q=2, p=P, n=BLK)
        w_gate_d = w_gate[0].rearrange("(h q k p) (b n) -> h q b p k n", h=2, q=2, p=P, n=BLK)
        w_out_d = w_out[0].rearrange("(h q k p) (b n) -> h q b p k n", h=2, q=2, p=P, n=BLK)
        w_br_d = [w[0].rearrange("(q k p) (b n) -> q b p k n", q=2, p=P, n=BLK)
                  for w in (w_br_diff, w_br_sb)]
        up_d = [w[0].rearrange("(g e) (k p) n -> k g p e n", e=SIDE, p=P) for w in (w_up_gate, w_up)]
        down_d = w_down[0].rearrange("(g u e) (f p) (h n) -> h f u g p e n", u=2, e=SIDE // 2, p=P, h=2)

        def slot(s):
            return ring[:, s].rearrange("p (k n) -> p k n", n=BLK)

        qkv_cols = qkv[:, :, :, :, :].rearrange("p t a (c h) d -> p t (a c) (h d)", c=2)
        gate_cols = gates[:, :, :].rearrange("p t (b n) -> p t b n", n=BLK)
        x_cols = x_tok[:, :, :].rearrange("p t (b n) -> p t b n", n=BLK)

        block = ctx.enter_context(nc.Block())

        @block.sync
        def _(sp):
            sp.sem_inc(slots_used, RING)
            for t in range(TT):
                sp.dma_start(x_tok[:, t], x_d[t]).then_inc(x_in, 16)

            def load(s, turn, quarters):
                sp.wait_ge(slots_used, RING * turn + s + 1)
                for q, src in enumerate(quarters):
                    dst = ring[:, s, q * 4 * BLK:(q + 1) * 4 * BLK]
                    dst = dst.rearrange("p (k n) -> p k n", k=src.shape[1])
                    sp.dma_start(dst, src).then_inc(slot_full[s], 16)

            with sp.Fori(0, TURN_GATE) as i:
                for s in range(RING):
                    load(s, i, [w_in_d[s % 2, q].rearrange("(i j) p k n -> i j p k n", j=PAIR)[i, s // 2]
                                for q in range(2)])
            with sp.Fori(0, GATE_BLOCKS // PAIR) as i:
                for s in range(RING):
                    load(s, i + TURN_GATE, [w_gate_d[s % 2, q].rearrange("(i j) p k n -> i j p k n", j=PAIR)[i, s // 2]
                                            for q in range(2)])
            for n in range(2 * OUT_BLOCKS):
                load(n % RING, TURN_BR + n // RING, [w_br_d[n % 2][q, n // 2] for q in range(2)])
            for n in range(2 * OUT_BLOCKS):
                load(n % RING, TURN_OUT + n // RING, [w_out_d[n % 2, q, n // 2] for q in range(2)])

            def load_experts(g, turn):
                for k in range(KD):
                    load(k % RING, turn + k // RING, [w[k, g] for w in up_d])
                for n in range(2 * (FF // P)):
                    load(n % RING, turn + (KD + n) // RING,
                         [down_d[n // (FF // P), n % (FF // P), u, g] for u in range(2)])

            with sp.Fori(0, GROUPS) as g:
                load_experts(g, g * MOE_TURNS + TURN_MOE)
            sp.wait_ge(passes_made, 1)
            passes = sp.value_load(passes_i[0:1, 0:1], min_val=1, max_val=MAX_PASSES)
            with sp.If(passes > 1):
                with sp.Fori(1, passes) as again:
                    with sp.Fori(0, GROUPS) as g:
                        load_experts(g, (again * GROUPS + g) * MOE_TURNS + TURN_MOE)
            for n in range(2 * TT):
                t, h = n // 2, n % 2
                sp.wait_ge(out_made, n + 1)
                sp.dma_start(out_d[t][:, h * (D // 2):(h + 1) * (D // 2)],
                             normed[:, t, h * (D // 2):(h + 1) * (D // 2)]).then_inc(out_written, 16)
            sp.wait_ge(out_written, 16 * 2 * TT)

        @block.gpsimd
        def _(pool):
            pool.sem_inc(qk_turned, 1)
            pool.memset(ident[:], 0.0)
            pool.memset(ones[:], 1.0)
            pool.memset(mask_upto[:], 0.0)
            pool.memset(mask_before[:], 0.0)
            for i in range(HALF):
                f = np.float32(ROPE_THETA) ** np.float32(-2.0 * i / (2 * HALF))
                pool.memset(inv_freq[:, i:i + 1], float(f))
            pool.iota(slot_id[:], [[1, SLOTS]], base=0, channel_multiplier=0,
                      allow_small_or_imprecise_dtypes=True)
            pool.iota(falling[:], [[-1, NE]], base=NE, channel_multiplier=0,
                      allow_small_or_imprecise_dtypes=True)
            pool.iota(starts[:], [[SLOTS, MAX_PASSES - 1]], base=SLOTS, channel_multiplier=0,
                      allow_small_or_imprecise_dtypes=True)
            pool.drain()
            pool.affine_select(out=ident[:], in_=ident[:], compare_op=ALU.not_equal, fill=1.0,
                               base=0, pattern=[[-1, P]], channel_multiplier=1)
            pool.affine_select(out=before[:], in_=ones[:], compare_op=ALU.is_ge, fill=0.0,
                               base=-1, pattern=[[1, P]], channel_multiplier=-1)
            for m, off in ((mask_upto, 0), (mask_before, -1)):
                for c in (0, 2 * P):
                    pool.affine_select(out=m[:, c:c + P], in_=m[:, c:c + P], compare_op=ALU.is_ge,
                                       fill=-BIG, base=off, pattern=[[-1, P]], channel_multiplier=1)
            pool.drain().then_inc(masks_made, 1)
            vec = lambda a: a.rearrange("a (k p) -> p (a k)", p=P)
            with nc.allow_non_contiguous_dma("small vectors"):
                pool.dma_start(g_mix_sb[:], vec(g_mix)).then_inc(consts_in, 16)
                pool.dma_start(pos_i[:], positions.rearrange("a (t p) -> p (a t)", p=P)).then_inc(consts_in, 16)
                pool.dma_start(lam_sb[:], lambda_params[0].partition_broadcast(P)).then_inc(consts_in, 16)
                pool.dma_start(gsub[:], g_subln[0].partition_broadcast(P)).then_inc(consts_in, 16)
                pool.dma_start(g_moe_sb[:], vec(g_moe)).then_inc(consts_in, 16)
                pool.dma_start(w_route[:, :, 0:NG], w_group[0].rearrange("(k p) n -> p k n", p=P)).then_inc(consts_in, 16)
                pool.dma_start(w_route[:, :, NG:], w_router[0].rearrange("(k p) n -> p k n", p=P)).then_inc(consts_in, 16)
                pool.dma_start(b_route[:, 0:NG], b_group[0].partition_broadcast(P)).then_inc(consts_in, 16)
                pool.dma_start(b_route[:, NG:], b_router[0].partition_broadcast(P)).then_inc(consts_in, 16)

            rope_blocks = 2 * HEADS * P // BLK
            pool.wait_ge(sines_made, 2)
            pool.wait_ge(proj_act, 2 + rope_blocks)
            pool.wait_ge(proj_dve, 2 + rope_blocks)
            for t in range(TT):
                qk = qkv[:, t, DQ:DK + 1, :, :].rearrange("p a h (c d) -> p (a h c) d", c=2)
                first, second = qk[:, :, 0:HALF], qk[:, :, HALF:2 * HALF]
                c = cos[:, t].unsqueeze(1).broadcast_to([P, 4 * HEADS, HALF])
                s = sin[:, t].unsqueeze(1).broadcast_to([P, 4 * HEADS, HALF])
                if t:
                    pool.drain()
                pool.tensor_tensor(rope_tmp[:, 0], first, c, ALU.mult)
                pool.tensor_tensor(rope_tmp[:, 1], second, s, ALU.mult)
                pool.tensor_tensor(rope_tmp[:, 2], second, c, ALU.mult)
                pool.tensor_tensor(rope_tmp[:, 3], first, s, ALU.mult)
                pool.drain()
                pool.tensor_tensor(first, rope_tmp[:, 0], rope_tmp[:, 1], ALU.subtract)
                pool.tensor_tensor(second, rope_tmp[:, 2], rope_tmp[:, 3], ALU.add)
            pool.drain()
            pool.wait_ge(proj_act, 2 + IN_BLOCKS)
            pool.wait_ge(proj_dve, 2 + IN_BLOCKS)

            def stage_head(head):
                pool.wait_ge(qk_turned, head + 1)
                for n, a in enumerate((DQ, DK, SQ, SK)):
                    pool.tensor_copy(stage[:, :, n], qkv[:, :, a].rearrange("p t h d -> p h t d")[:, head])
                pool.drain().then_inc(staged, 1)

            with pool.Fori(0, HEADS) as head:
                stage_head(head)

            pool.wait_ge(x_added, OUT_BLOCKS)
            pool.dma_start(g_final_sb, g_final.partition_broadcast(P)).then_inc(g_final_in, 16)

        @block.tensor
        def _(pe):
            def turn_chunks(src, first):
                for m in range(KH):
                    if m >= 4:
                        pe.wait_ge((turned_act, turned_dve)[m % 2], first * KH + 2 * ((m - 4) // 2 + 1))
                    for k in range(2):
                        for t in range(TT):
                            c = k * T + t * P
                            mm = pe.transpose(bank[4 + m % 4][:, c:c + P], src(2 * m + k, t), ident[:])
                    mm.then_inc(turned, 1)

            def project(n, j, turn, quarters):
                for half in range(2):
                    s = 2 * j + half
                    for q in range(2):
                        if half == 0 and q == 0:
                            pe.wait_ge(proj_act, n + 1)
                            pe.wait_ge(proj_dve, n + 1)
                        if q == 0:
                            pe.wait_ge(slot_full[s], 32 * (turn + 1))
                        for k in range(4 * q, 4 * q + 4):
                            for t in range(TT):
                                mm = pe.matmul(bank[2 * j + t][:], hT[:, KH * half + k, t * P:(t + 1) * P],
                                               slot(s)[:, k], start=(half == 0 and k == 0),
                                               stop=(half == 1 and k == KH - 1))
                        if q == 1:
                            mm.then_inc(slots_used, 1)
                        quarters(2 * half + q)

            pe.wait_ge(masks_made, 1)
            pe.wait_ge(normed_act, 1)
            pe.wait_ge(normed_dve, 1)
            turn_chunks(lambda k, t: normed[:, t, k * P:(k + 1) * P], 0)
            pe.wait_ge(turned_act, KH)
            pe.wait_ge(turned_dve, KH)
            with pe.Fori(0, TURN_GATE) as i:
                for j in range(PAIR):
                    project(i * PAIR + j, j, i, lambda q: None)

            def attend(head, step):
                if step == 0:
                    pe.wait_ge(qkT_act, head + 1)
                    pe.wait_ge(qkT_dve, head + 1)
                    pe.wait_ge(heads_stored, head + 1)
                    for m in range(2):
                        r = slice(m * HQ, (m + 1) * HQ)
                        pe.matmul(bank[6 + m][:, 0:P], qkT[r, 0, 0:P], qkT[r, 1, 0:P], start=True, stop=True)
                        mm = pe.matmul(bank[6 + m][:, P:3 * P], qkT[r, 0, P:T], qkT[r, 1, :], start=True, stop=True)
                    mm.then_inc(diff_scored, 1)
                    pe.matmul(bank[4][:, 0:P], qkT[:, 2, 0:P], qkT[:, 3, 0:P], start=True, stop=True)
                    pe.matmul(bank[4][:, P:3 * P], qkT[:, 2, P:T], qkT[:, 3, :],
                              start=True, stop=True).then_inc(sb_scored, 1)
                if step == 2:
                    pe.wait_ge(diff_made, head + 1)
                    for c in range(3):
                        mm = pe.transpose(bank[5][:, c * P:(c + 1) * P], diff[:, c * P:(c + 1) * P], ident[:])
                    mm.then_inc(diff_turned, 1)
                    pe.wait_ge(stick_exped, head + 1)
                    for c in range(3):
                        mm = pe.transpose(bank[6][:, c * P:(c + 1) * P], stick[:, c * P:(c + 1) * P], ident[:])
                    mm.then_inc(sb_turned, 1)
                if step == 3:
                    pe.wait_ge(aT_act, head + 1)
                    pe.wait_ge(aT_dve, head + 1)
                    for n, (aT, a) in enumerate(((aT_diff, DV), (aT_sb, SV))):
                        v = [qkv[:, t, a][:, head] for t in range(TT)]
                        o = bank[7][:, n * T:(n + 1) * T]
                        pe.matmul(o[:, 0:P], aT[:, 0:P], v[0], start=True, stop=True)
                        pe.matmul(o[:, P:T], aT[:, P:2 * P], v[0], start=True, stop=False)
                        mm = pe.matmul(o[:, P:T], aT[:, 2 * P:3 * P], v[1], start=False, stop=True)
                    mm.then_inc(heads_out, 1)

            with pe.Fori(0, GATE_BLOCKS // PAIR) as i:
                for j in range(PAIR):
                    head = i * PAIR + j
                    pe.wait_ge(staged, head + 1)
                    for n in range(4):
                        for t in range(TT):
                            c = (n % 2) * T + t * P
                            mm = pe.transpose(bank[4 + n // 2][:, c:c + P], stage[:, t, n], ident[:])
                    mm.then_inc(qk_turned, 1)
                    project(head + IN_BLOCKS, j, i + TURN_GATE, lambda q: attend(head, q))

            pe.wait_ge(heads_stored, HEADS + 1)
            turn_chunks(lambda k, t: qkv[:, t, (DQ, SQ)[k // HEADS], k % HEADS], 1)
            pe.wait_ge(turned_act, 2 * KH)
            pe.wait_ge(turned_dve, 2 * KH)
            pe.wait_ge(proj_act, 2 + IN_BLOCKS + GATE_BLOCKS)
            pe.wait_ge(proj_dve, 2 + IN_BLOCKS + GATE_BLOCKS)

            def turn_mixed(n):
                pe.wait_ge(mixed, 2 * n + 2)
                for c in range(2):
                    if n:
                        pe.wait_ge(mixT_made, 2 * n + c - 1)
                    for k in range(2):
                        for t in range(TT):
                            at = (2 * c + k) * P
                            mm = pe.transpose(bank[6 + c][:, k * T + t * P:k * T + (t + 1) * P],
                                              gate_cols[:, t, n, at:at + P], ident[:])
                    mm.then_inc(mix_turned, 1)

            for n in range(2 * OUT_BLOCKS):
                pair = 2 * (n % 3)
                if n >= 3:
                    pe.wait_ge(mixed, n - 2)
                pe.wait_ge(slot_full[n % RING], 32 * (TURN_BR + n // RING + 1))
                for k in range(KH):
                    for t in range(TT):
                        mm = pe.matmul(bank[pair + t][:], hT[:, KH * (n % 2) + k, t * P:(t + 1) * P],
                                       slot(n % RING)[:, k], start=(k == 0), stop=(k == KH - 1))
                mm.then_inc(slots_used, 1)
                if n % 2 and n > 1:
                    turn_mixed(n // 2 - 1)
            turn_mixed(OUT_BLOCKS - 1)
            pe.wait_ge(mixT_made, 2 * OUT_BLOCKS)
            for n in range(OUT_BLOCKS):
                pair = 2 * (n % 2)
                if n >= 2:
                    pe.wait_ge(x_added, n - 1)
                for half in range(2):
                    m = 2 * n + half
                    pe.wait_ge(slot_full[m % RING], 32 * (TURN_OUT + m // RING + 1))
                    for k in range(KH):
                        for t in range(TT):
                            mm = pe.matmul(bank[pair + t][:], mixT[:, KH * half + k, t * P:(t + 1) * P],
                                           slot(m % RING)[:, k], start=(half == 0 and k == 0),
                                           stop=(half == 1 and k == KH - 1))
                    mm.then_inc(slots_used, 1)

            pe.wait_ge(normed_act, 2)
            pe.wait_ge(normed_dve, 2)
            turn_chunks(lambda k, t: normed[:, t, k * P:(k + 1) * P], 2)
            pe.wait_ge(turned_act, 3 * KH)
            pe.wait_ge(turned_dve, 3 * KH)
            pe.wait_ge(x_added, OUT_BLOCKS)
            NR = NG + NE
            for t in range(TT):
                for k in range(KD):
                    mm = pe.matmul(bank[0][:, t * NR:(t + 1) * NR], hT[:, k, t * P:(t + 1) * P],
                                   w_route[:, k], start=(k == 0), stop=(k == KD - 1))
            mm.then_inc(logits_made, 1)
            pe.wait_ge(chosen_made, 1)
            for t in range(TT):
                for u in range(t + 1):
                    pe.matmul(bank[1][:, t * NE:(t + 1) * NE], (before if u == t else ones)[:],
                              chosen[:, u], start=(u == 0), stop=(u == t))
            for u in range(TT):
                mm = pe.matmul(bank[1][:, TT * NE:(TT + 1) * NE], ones[:], chosen[:, u],
                               start=(u == 0), stop=(u == TT - 1))
            mm.then_inc(ranks_made, 1)

            def experts(m):
                turn = m * MOE_TURNS + TURN_MOE
                pe.wait_ge(picks_made, m + 1)
                pe.wait_ge(added, m * 2 * TT * 2 + 1)
                for q in range(4):
                    if q >= 2:
                        pe.wait_ge(xg_made, m * 4 + q - 1)
                    for k in range(4):
                        for t in range(TT):
                            mm = pe.matmul(bank[2 + q % 2][:, k * P:(k + 1) * P],
                                           normed[:, t, (4 * q + k) * P:(4 * q + k + 1) * P],
                                           pick[:, 0, t], start=(t == 0), stop=(t == TT - 1))
                    mm.then_inc(gathered, 1)
                for t in range(TT):
                    mm = pe.transpose(bank[5][:, t * P:(t + 1) * P], pick[:, 1, t], ident[:])
                mm.then_inc(place_turned, 1)
                for k in range(KD):
                    s = k % RING
                    if k % 4 == 0:
                        pe.wait_ge(xg_made, m * 4 + k // 4 + 1)
                    pe.wait_ge(slot_full[s], (turn + (k // RING + 1)) * 32)
                    for w in range(2):
                        for j in range(SIDE):
                            c = slice(j * SLOTS, (j + 1) * SLOTS)
                            mm = pe.matmul(bank[w][c, :], xgT[:, k, c], slot(s)[:, 4 * w + j],
                                           start=(k == 0), stop=(k == KD - 1),
                                           tile_position=(0, j * SLOTS))
                    mm.then_inc(slots_used, 1)
                pe.wait_ge(act_made, m + 1)
                for f in range(FF // P):
                    mm = pe.transpose(bank[4][:, f * P:(f + 1) * P], act_sb[:, 1, f * P:(f + 1) * P], ident[:])
                mm.then_inc(act_turned, 1)
                pe.wait_ge(actT_made, m + 1)
                pe.wait_ge(placeT_made, m + 1)
                for n in range(2 * (FF // P)):
                    half, f = n // (FF // P), n % (FF // P)
                    s = n % RING
                    pe.wait_ge(slot_full[s], (turn + ((KD + n) // RING + 1)) * 32)
                    for b in range(2):
                        for j in range(SIDE):
                            c = slice(j * SLOTS, (j + 1) * SLOTS)
                            mm = pe.matmul(bank[4 + 2 * half + b][c, :], actT[:, f, c], slot(s)[:, 2 * j + b],
                                           start=(f == 0), stop=(f == FF // P - 1),
                                           tile_position=(0, j * SLOTS))
                    mm.then_inc(slots_used, 1)
                pe.wait_ge(y_act, m * 2 + 2)
                pe.wait_ge(y_dve, m * 2 + 2)
                for n in range(4 * TT):
                    b, t = n // TT, n % TT
                    if n >= 2:
                        pe.wait_ge(added, m * (4 * TT) + n)
                    pe.matmul(bank[2 + n % 2][:], placeT[:, t * P:(t + 1) * P],
                              y_sb[:, b * BLK:(b + 1) * BLK], start=True, stop=True).then_inc(combined, 1)

            with pe.Fori(0, GROUPS) as g:
                experts(g)
            pe.wait_ge(passes_made, 1)
            passes = pe.value_load(passes_i[0:1, 0:1], min_val=1, max_val=MAX_PASSES)
            with pe.If(passes > 1):
                with pe.Fori(1, passes) as again:
                    with pe.Fori(0, GROUPS) as g:
                        experts(again * GROUPS + g)

        @block.scalar
        def _(act):
            act.sem_inc(proj_act, 2)

            def guess_rstd(n):
                act.wait_ge(var_made, n + 1)
                act.activation(rstd[:], var[:], ACT.Ln)
                act.drain()
                act.activation(rstd[:], rstd[:], ACT.Exp, scale=-0.5)
                act.drain().then_inc(rstd_guess, 1)

            def copy_turned(first, scale):
                for m in range(0, KH, 2):
                    act.wait_ge(turned, first * KH + m + 1)
                    for k in range(2):
                        src, chunk = bank[4 + m % 4][:, k * T:(k + 1) * T], 2 * m + k
                        if scale is None:
                            act.activation(hT[:, chunk], src, ACT.Copy).then_inc(turned_act, 1)
                        else:
                            act.activation(hT[:, chunk], src, ACT.Copy,
                                           scale=scale[:, chunk:chunk + 1]).then_inc(turned_act, 1)

            for t in range(TT):
                act.wait_ge(x_in, 16 * TT)
                if t:
                    act.drain()
                act.activation(junk, x_tok[:, t], ACT.Square, accum_out=ssq[:, t, 0:1])
            act.drain().then_inc(squared, 1)
            guess_rstd(0)
            act.wait_ge(lam_summed, 1)
            act.activation(lam_two[:], lam_two[:], ACT.Exp).then_inc(lam_exped, 1)
            act.wait_ge(rstd_made, 1)
            act.activation(normed[:, 0], x_tok[:, 0], ACT.Copy, scale=rstd[:, 0:1]).then_inc(normed_act, 1)
            act.wait_ge(consts_in, 16 * 9)
            copy_turned(0, g_mix_sb)
            act.wait_ge(angles_made, 1)
            act.activation(sin[:], angle[:], ACT.Sin).then_inc(sines_made, 1)
            act.activation(cos[:], angle[:], ACT.Sin, scale=0.5).then_inc(angles_made, 1)

            def copy_block(n, j, dst):
                act.wait_ge(slots_used, (n + 1) * 2 + RING)
                act.activation(dst, bank[2 * j][:], ACT.Copy).then_inc(proj_act, 1)

            with act.Fori(0, TURN_GATE) as i:
                for j in range(PAIR):
                    dst = qkv_cols[:, 0].rearrange("p (i j) n -> p i j n", j=PAIR)[:, i, j]
                    copy_block(i * PAIR + j, j, dst)

            with act.Fori(0, GATE_BLOCKS // PAIR) as i:
                for j in range(PAIR):
                    head = i * PAIR + j
                    act.wait_ge(qk_turned, head + 2)
                    act.activation(qkT[:, 0:2], bank[4][:], ACT.Copy).then_inc(qkT_act, 1)
                    act.wait_ge(tops_made, head + 1)
                    for t in range(TT):
                        for m in range(2):
                            p_ = prob[:, m, 0:P] if t == 0 else prob[:, m, P:3 * P]
                            act.activation(p_, p_, ACT.Exp, bias=neg_top[:, t, m:m + 1],
                                           accum_out=total[:, t, m:m + 1])
                    act.drain().then_inc(diff_exped, 1)
                    act.wait_ge(z_made, head + 1)
                    act.activation(soft[:], z[:], ACT.Abs)
                    act.drain()
                    act.activation(soft[:], soft[:], ACT.Exp, scale=-1.0)
                    act.drain()
                    act.activation(soft[:], soft[:], ACT.Ln, bias=1.0).then_inc(soft_made, 1)
                    act.wait_ge(stick_summed, head + 1)
                    act.activation(stick[:], stick[:], ACT.Exp).then_inc(stick_exped, 1)
                    act.wait_ge(diff_turned, head + 1)
                    act.activation(aT_diff[:], bank[5][:, 0:3 * P], ACT.Copy).then_inc(aT_act, 1)
                    act.wait_ge(heads_out, head + 1)
                    for t in range(TT):
                        act.activation(soft[:, t * P:(t + 1) * P], bank[7][:, t * P:(t + 1) * P],
                                       ACT.Square, accum_out=ssq[:, t, 0:1])
                    act.drain().then_inc(head_squared, 1)
                    act.wait_ge(head_var, head + 1)
                    act.activation(rstd[:], var[:], ACT.Ln)
                    act.drain()
                    act.activation(rstd[:], rstd[:], ACT.Exp, scale=-0.5).then_inc(head_guess, 1)
                    copy_block(head + IN_BLOCKS, j,
                               gate_cols[:, 0].rearrange("p (i j) n -> p i j n", j=PAIR)[:, i, j])

            copy_turned(1, None)
            act.wait_ge(proj_dve, 2 + IN_BLOCKS + GATE_BLOCKS)
            for t in range(TT):
                act.activation(gates[:, t], gates[:, t], ACT.Sigmoid)
            act.drain().then_inc(gates_open, 1)
            for n in range(2 * OUT_BLOCKS):
                act.wait_ge(mix_turned, n + 1)
                act.activation(mixT[:, 2 * n:2 * n + 2].rearrange("p a b -> p (a b)"), bank[6 + n % 2][:],
                               ACT.Copy).then_inc(mixT_made, 1)
            for n in range(OUT_BLOCKS):
                act.wait_ge(x_added, n + 1)
                for t in range(TT):
                    act.activation(junk[:, (n * TT + t) % 4 * BLK:((n * TT + t) % 4 + 1) * BLK], x_cols[:, t, n],
                                   ACT.Square, accum_out=ssq[:, t, n:n + 1])
                act.drain()
            act.drain().then_inc(squared, 1)
            guess_rstd(1)
            act.wait_ge(rstd_made, 2)
            act.activation(normed[:, 0], x_tok[:, 0], ACT.Copy, scale=rstd[:, 0:1]).then_inc(normed_act, 1)
            copy_turned(2, g_moe_sb)
            act.wait_ge(route_shifted, 1)
            act.activation(shifted, shifted, ACT.Exp).then_inc(route_exped, 1)

            def experts(m):
                act.wait_ge(place_turned, m + 2)
                act.activation(placeT, bank[5][:, 0:T], ACT.Copy).then_inc(placeT_made, 1)
                act.wait_ge(slots_used, m * (MOE_TURNS * RING) + (RING + USED_MOE + KD))
                act.activation(act_sb[:, 0], bank[0][:], ACT.Silu).then_inc(silu_made, 1)
                act.wait_ge(act_turned, m + 1)
                act.activation(actT.rearrange("p a b -> p (a b)"), bank[4][:], ACT.Copy).then_inc(actT_made, 1)
                for half in range(2):
                    act.wait_ge(slots_used, m * (MOE_TURNS * RING) + (RING + USED_MOE + KD + (half + 1) * (FF // P)))
                    act.activation(y_sb[:, 2 * half * BLK:(2 * half + 1) * BLK], bank[4 + 2 * half][:],
                                   ACT.Copy).then_inc(y_act, 1)

            with act.Fori(0, GROUPS) as g:
                experts(g)
            act.wait_ge(passes_made, 1)
            passes = act.value_load(passes_i[0:1, 0:1], min_val=1, max_val=MAX_PASSES)
            with act.If(passes > 1):
                with act.Fori(1, passes) as again:
                    with act.Fori(0, GROUPS) as g:
                        experts(again * GROUPS + g)
            act.wait_ge(x_final, 1)
            for t in range(TT):
                act.drain()
                act.activation(junk, x_tok[:, t], ACT.Square, accum_out=ssq[:, t, 0:1])
            act.drain().then_inc(squared, 1)
            guess_rstd(2)

        @block.vector
        def _(dve):
            dve.sem_inc(proj_dve, 2)
            dve.sem_inc(heads_stored, 1)
            dve.sem_inc(added, 1)
            dve.sem_inc(place_turned, 1)

            def newton_step(count_sem, n):
                dve.wait_ge(count_sem, n)
                dve.tensor_tensor(newton[:], rstd[:], rstd[:], ALU.mult)
                dve.drain()
                dve.tensor_tensor(newton[:], newton[:], var[:], ALU.mult)
                dve.drain()
                dve.tensor_scalar(newton[:], newton[:], -0.5, 1.5, ALU.mult, ALU.add)
                dve.drain()
                dve.tensor_tensor(rstd[:], rstd[:], newton[:], ALU.mult)
                dve.drain()

            def norm(n, parts):
                dve.wait_ge(squared, n + 1)
                if parts > 1:
                    dve.tensor_reduce(var[:], ssq[:, :, 0:parts], AX, ALU.add)
                    dve.drain()
                    dve.tensor_scalar(var[:], var[:], 1.0 / D, EPS, ALU.mult, ALU.add).then_inc(var_made, 1)
                else:
                    dve.tensor_scalar(var[:], ssq[:, :, 0], 1.0 / D, EPS, ALU.mult, ALU.add).then_inc(var_made, 1)
                newton_step(rstd_guess, n + 1)

            def copy_turned(first, scale):
                for m in range(1, KH, 2):
                    dve.wait_ge(turned, first * KH + m + 1)
                    for k in range(2):
                        src, chunk = bank[4 + m % 4][:, k * T:(k + 1) * T], 2 * m + k
                        if scale is None:
                            dve.tensor_copy(hT[:, chunk], src).then_inc(turned_dve, 1)
                        else:
                            dve.tensor_scalar(hT[:, chunk], src, scale[:, chunk:chunk + 1], None,
                                              ALU.mult).then_inc(turned_dve, 1)

            norm(0, 1)
            dve.sem_inc(rstd_made, 1)
            dve.tensor_scalar(normed[:, 1], x_tok[:, 1], rstd[:, 1:2], None, ALU.mult).then_inc(normed_dve, 1)
            dve.wait_ge(consts_in, 16 * 9)
            lam_prod = stick[:, 0:2 * HQ].rearrange("p (a b) -> p a b", a=2)
            lam_v = lam_sb[:, :, :].rearrange("p (a b) d -> p a b d", b=2)
            dve.tensor_tensor(lam_prod, lam_v[:, :, 0], lam_v[:, :, 1], ALU.mult)
            dve.drain()
            dve.tensor_reduce(lam_two[:], lam_prod, AX, ALU.add).then_inc(lam_summed, 1)
            copy_turned(0, g_mix_sb)
            dve.wait_ge(lam_exped, 1)
            dve.tensor_scalar(neg_lam[:], lam_two[:, 0:1], -1.0, -LAMBDA_INIT, ALU.mult, ALU.add)
            dve.drain()
            dve.tensor_tensor(neg_lam[:], neg_lam[:], lam_two[:, 1:2], ALU.add)
            dve.tensor_scalar(gsub[:], gsub[:], 1.0 - LAMBDA_INIT, None, ALU.mult)
            dve.wait_ge(masks_made, 1)
            dve.tensor_copy(pos_f[:], pos_i[:])
            dve.drain()
            for t in range(TT):
                dve.tensor_scalar(angle[:, t], inv_freq[:], pos_f[:, t:t + 1], None, ALU.mult)
            dve.drain()
            dve.tensor_scalar(whole[:], angle[:], float(1 / (2 * np.pi)), None, ALU.mult)
            dve.drain()
            dve.tensor_scalar(whole[:], whole[:], ROUND, None, ALU.add)
            dve.drain()
            dve.tensor_scalar(whole[:], whole[:], -ROUND, None, ALU.add)
            for c in TWO_PI:
                dve.drain()
                dve.scalar_tensor_tensor(out=angle[:], in0=whole[:], scalar=-c, in1=angle[:],
                                         op0=ALU.mult, op1=ALU.add)
            dve.drain()
            dve.tensor_scalar(angle[:], angle[:], 3.1415925, -3.1415925, ALU.min, ALU.max).then_inc(angles_made, 1)
            dve.wait_ge(angles_made, 2)
            dve.tensor_tensor(cos[:], cos[:], cos[:], ALU.mult)
            dve.drain()
            dve.tensor_scalar(cos[:], cos[:], -2.0, 1.0, ALU.mult, ALU.add)
            dve.drain()
            dve.wait_ge(sines_made, 1)
            dve.sem_inc(sines_made, 1)

            def copy_block(n, j, dst):
                dve.wait_ge(slots_used, (n + 1) * 2 + RING)
                dve.tensor_copy(dst, bank[2 * j + 1][:]).then_inc(proj_dve, 1)

            with dve.Fori(0, TURN_GATE) as i:
                for j in range(PAIR):
                    copy_block(i * PAIR + j, j, qkv_cols[:, 1].rearrange("p (i j) n -> p i j n", j=PAIR)[:, i, j])

            with dve.Fori(0, GATE_BLOCKS // PAIR) as i:
                for j in range(PAIR):
                    head = i * PAIR + j
                    dve.wait_ge(qk_turned, head + 2)
                    dve.tensor_copy(qkT[:, 2:4].rearrange("p a b -> p (a b)"), bank[5][:]).then_inc(qkT_dve, 1)
                    dve.wait_ge(diff_scored, head + 1)
                    for m in range(2):
                        dve.scalar_tensor_tensor(out=prob[:, m], in0=bank[6 + m][:, 0:3 * P], scalar=HQ ** -0.5,
                                                 in1=mask_upto[:], op0=ALU.mult, op1=ALU.add)
                    dve.drain()
                    dve.tensor_reduce(top[:, 0], prob[:, :, 0:P], AX, ALU.max)
                    dve.tensor_reduce(top[:, 1], prob[:, :, P:3 * P], AX, ALU.max)
                    dve.drain()
                    dve.tensor_scalar(neg_top[:], top[:], -1.0, None, ALU.mult).then_inc(tops_made, 1)
                    dve.wait_ge(sb_scored, head + 1)
                    dve.scalar_tensor_tensor(out=z[:], in0=bank[4][:, 0:3 * P], scalar=P ** -0.5,
                                             in1=mask_before[:], op0=ALU.mult, op1=ALU.add).then_inc(z_made, 1)
                    dve.wait_ge(diff_exped, head + 1)
                    dve.reciprocal(weight[:], total[:])
                    dve.drain()
                    dve.tensor_scalar(weight[:, :, 1], weight[:, :, 1], neg_lam[:], None, ALU.mult)
                    for t in range(TT):
                        c = slice(0, P) if t == 0 else slice(P, 3 * P)
                        dve.tensor_scalar(diff[:, c], prob[:, 0, c], weight[:, t, 0:1], None, ALU.mult)
                    dve.drain()
                    for t in range(TT):
                        c = slice(0, P) if t == 0 else slice(P, 3 * P)
                        dve.scalar_tensor_tensor(out=diff[:, c], in0=prob[:, 1, c], scalar=weight[:, t, 1:2],
                                                 in1=diff[:, c], op0=ALU.mult, op1=ALU.add)
                    dve.drain().then_inc(diff_made, 1)
                    dve.wait_ge(soft_made, head + 1)
                    dve.scalar_tensor_tensor(out=soft[:], in0=z[:], scalar=0.0, in1=soft[:],
                                             op0=ALU.max, op1=ALU.add)
                    dve.drain()
                    for c in (slice(0, P), slice(P, 3 * P)):
                        dve.tensor_tensor_scan(stick[:, c][:, ::-1], soft[:, c][:, ::-1], soft[:, c][:, ::-1],
                                               0.0, ALU.add, ALU.max)
                    dve.drain()
                    dve.tensor_tensor(stick[:], z[:], stick[:], ALU.subtract).then_inc(stick_summed, 1)
                    dve.wait_ge(sb_turned, head + 1)
                    dve.tensor_copy(aT_sb[:], bank[6][:, 0:3 * P]).then_inc(aT_dve, 1)
                    dve.wait_ge(head_squared, head + 1)
                    dve.tensor_scalar(var[:], ssq[:, :, 0], 1.0 / HV, EPS, ALU.mult, ALU.add).then_inc(head_var, 1)
                    dve.tensor_copy(qkv[:, :, SQ].rearrange("p t h d -> p h t d")[:, head],
                                    bank[7][:, T:2 * T].rearrange("p (t d) -> p t d", t=TT))
                    newton_step(head_guess, head + 1)
                    for t in range(TT):
                        dve.scalar_tensor_tensor(out=qkv[:, t, DQ][:, head], in0=bank[7][:, t * P:(t + 1) * P],
                                                 scalar=rstd[:, t:t + 1], in1=gsub[:], op0=ALU.mult, op1=ALU.mult)
                    dve.drain()
                    dve.sem_inc(heads_stored, 1)
                    copy_block(head + IN_BLOCKS, j,
                               gate_cols[:, 1].rearrange("p (i j) n -> p i j n", j=PAIR)[:, i, j])

            copy_turned(1, None)
            dve.wait_ge(gates_open, 1)
            for n in range(2 * OUT_BLOCKS):
                pair = 2 * (n % 3)
                dve.wait_ge(slots_used, RING * (TURN_BR + 1) + n + 1)
                for t in range(TT):
                    g = gate_cols[:, t, (n % 2) * OUT_BLOCKS + n // 2]
                    dve.tensor_tensor(g, g, bank[pair + t][:], ALU.mult)
                dve.drain()
                if n % 2 == 0:
                    dve.sem_inc(mixed, 1)
                else:
                    for t in range(TT):
                        g0, g1 = gate_cols[:, t, n // 2], gate_cols[:, t, OUT_BLOCKS + n // 2]
                        dve.tensor_tensor(g0, g0, g1, ALU.add)
                    dve.drain().then_inc(mixed, 1)
            for n in range(OUT_BLOCKS):
                pair = 2 * (n % 2)
                dve.wait_ge(slots_used, RING * (TURN_OUT + 1) + 2 * n + 2)
                for t in range(TT):
                    dve.tensor_tensor(x_cols[:, t, n], x_cols[:, t, n], bank[pair + t][:], ALU.add)
                dve.drain().then_inc(x_added, 1)
            norm(1, OUT_BLOCKS)
            dve.sem_inc(rstd_made, 1)
            dve.tensor_scalar(normed[:, 1], x_tok[:, 1], rstd[:, 1:2], None, ALU.mult).then_inc(normed_dve, 1)
            copy_turned(2, g_moe_sb)

            def bc(v, n):
                return v.broadcast_to([P, TT, n])

            def first_max(out_, values, top_, n):
                dve.tensor_tensor(out_, values, bc(top_, n), ALU.is_equal)
                dve.drain()
                fall = falling[:, NE - n:NE].unsqueeze(1).broadcast_to([P, TT, n])
                dve.tensor_tensor(tie[:, :, 0:n], out_, fall, ALU.mult)
                dve.drain()
                dve.tensor_reduce(tie_top, tie[:, :, 0:n], AX, ALU.max)
                dve.drain()
                dve.tensor_tensor(out_, tie[:, :, 0:n], bc(tie_top, n), ALU.is_equal)
                dve.drain()

            dve.wait_ge(logits_made, 1)
            dve.tensor_tensor(logits, bank[0][:, 0:TT * (NG + NE)].rearrange("p (t n) -> p t n", t=TT),
                              b_route[:].unsqueeze(1).broadcast_to([P, TT, NG + NE]), ALU.add)
            dve.drain()
            dve.tensor_reduce(best[:, :, 0:1], logits[:, :, 0:NG], AX, ALU.max)
            dve.drain()
            first_max(is_group, logits[:, :, 0:NG], best[:, :, 0:1], NG)
            dve.tensor_tensor(shifted[:, :, 0:NG], logits[:, :, 0:NG], bc(best[:, :, 0:1], NG), ALU.subtract)
            dve.tensor_scalar(is_group, is_group, BIG, -BIG, ALU.mult, ALU.add)
            dve.drain()
            for t in range(TT):
                dve.tensor_tensor(masked[:, t].rearrange("p (g e) -> p g e", g=NG),
                                  logits[:, t, NG:].rearrange("p (g e) -> p g e", g=NG),
                                  is_group[:, t].unsqueeze(2).broadcast_to([P, NG, PER]), ALU.add)
            dve.drain()
            for c in range(2):
                dve.tensor_reduce(best[:, :, 1 + c:2 + c], masked, AX, ALU.max)
                dve.drain()
                first_max(is_top[c], masked, best[:, :, 1 + c:2 + c], NE)
                if c == 0:
                    dve.scalar_tensor_tensor(out=masked, in0=is_top[0], scalar=-2 * BIG, in1=masked,
                                             op0=ALU.mult, op1=ALU.add)
                    dve.drain()
            dve.tensor_tensor(shifted[:, :, NG:NG + 1], best[:, :, 2:3], best[:, :, 1:2], ALU.subtract)
            dve.tensor_tensor(chosen, is_top[0], is_top[1], ALU.add)
            dve.drain().then_inc(route_shifted, 1)
            dve.sem_inc(chosen_made, 1)
            dve.wait_ge(route_exped, 1)
            dve.tensor_reduce(pair_w[:, :, 0:1], shifted[:, :, 0:NG], AX, ALU.add)
            dve.tensor_scalar(pair_w[:, :, 1:2], shifted[:, :, NG:NG + 1], 1.0, None, ALU.add)
            dve.drain()
            dve.reciprocal(pair_w[:, :, 0:2], pair_w[:, :, 0:2])
            dve.drain()
            dve.tensor_tensor(pair_w[:, :, 3:4], pair_w[:, :, 1:2], shifted[:, :, NG:NG + 1], ALU.mult)
            dve.drain()
            dve.tensor_tensor(pair_w[:, :, 2:3], pair_w[:, :, 1:2], pair_w[:, :, 0:1], ALU.mult)
            dve.tensor_tensor(pair_w[:, :, 3:4], pair_w[:, :, 3:4], pair_w[:, :, 0:1], ALU.mult)
            dve.drain()
            for c in range(2):
                dve.tensor_tensor(is_top[c], is_top[c], bc(pair_w[:, :, 2 + c:3 + c], NE), ALU.mult)
            dve.drain()
            dve.tensor_tensor(combine, is_top[0], is_top[1], ALU.add)
            dve.wait_ge(ranks_made, 1)
            dve.scalar_tensor_tensor(out=rank, in0=bank[1][:, 0:TT * NE].rearrange("p (t n) -> p t n", t=TT),
                                     scalar=float(2 * T), in1=chosen, op0=ALU.add, op1=ALU.mult)
            dve.tensor_reduce(count[:, 0:1], bank[1][:, TT * NE:(TT + 1) * NE], AX, ALU.max)
            dve.drain()
            dve.tensor_scalar(rank, rank, -float(2 * T), None, ALU.add)
            dve.tensor_scalar(over, starts[:], count[:, 0:1], None, ALU.is_lt)
            dve.drain()
            dve.tensor_reduce(count[:, 1:2], over, AX, ALU.add)
            dve.drain()
            dve.tensor_scalar(count[:, 1:2], count[:, 1:2], 1.0, None, ALU.add)
            dve.drain()
            dve.tensor_copy(passes_i[:], count[:, 1:2])
            dve.drain().then_inc(passes_made, 1)

            def experts(m, g):
                dve.drain()
                dve.wait_ge(place_turned, m + 1)
                for t in range(TT):
                    by_expert = lambda v: (v[:, t].rearrange("p (g e) -> p g e", e=SIDE)[:, g]
                                           .unsqueeze(2).broadcast_to([P, SIDE, SLOTS]))
                    hot = pick[:, 0, t].rearrange("p (e s) -> p e s", e=SIDE)
                    dve.tensor_tensor(hot, slot_id[:].unsqueeze(1).broadcast_to([P, SIDE, SLOTS]),
                                      by_expert(rank), ALU.is_equal)
                dve.drain()
                for t in range(TT):
                    by_expert = lambda v: (v[:, t].rearrange("p (g e) -> p g e", e=SIDE)[:, g]
                                           .unsqueeze(2).broadcast_to([P, SIDE, SLOTS]))
                    dve.tensor_tensor(pick[:, 1, t].rearrange("p (e s) -> p e s", e=SIDE),
                                      pick[:, 0, t].rearrange("p (e s) -> p e s", e=SIDE),
                                      by_expert(combine), ALU.mult)
                dve.drain()
                dve.sem_inc(picks_made, 1)
                for q in range(4):
                    dve.wait_ge(gathered, m * 4 + q + 1)
                    dve.tensor_tensor(xgT[:, 4 * q:4 * q + 4], bank[2 + q % 2][:].rearrange("p (k s) -> p k s", k=4),
                                      g_moe_sb[:, 4 * q:4 * q + 4].unsqueeze(2).broadcast_to([P, 4, P]),
                                      ALU.mult).then_inc(xg_made, 1)
                dve.wait_ge(silu_made, m + 1)
                dve.tensor_tensor(act_sb[:, 1], act_sb[:, 0], bank[1][:], ALU.mult).then_inc(act_made, 1)
                for half in range(2):
                    dve.wait_ge(slots_used, m * (MOE_TURNS * RING) + (RING + USED_MOE + KD + (half + 1) * (FF // P)))
                    dve.tensor_copy(y_sb[:, (2 * half + 1) * BLK:(2 * half + 2) * BLK],
                                    bank[5 + 2 * half][:]).then_inc(y_dve, 1)
                for n in range(4 * TT):
                    b, t = n // TT, n % TT
                    dve.wait_ge(combined, m * (4 * TT) + n + 1)
                    dve.tensor_tensor(x_cols[:, t, b], x_cols[:, t, b], bank[2 + n % 2][:],
                                      ALU.add).then_inc(added, 1)

            with dve.Fori(0, GROUPS) as g:
                experts(g, g)
            passes = dve.value_load(passes_i[0:1, 0:1], min_val=1, max_val=MAX_PASSES)
            with dve.If(passes > 1):
                with dve.Fori(1, passes) as again:
                    dve.drain()
                    dve.tensor_scalar(rank, rank, -float(SLOTS), None, ALU.add)
                    dve.drain()
                    with dve.Fori(0, GROUPS) as g:
                        experts(again * GROUPS + g, g)
            dve.drain().then_inc(x_final, 1)

            norm(2, 1)
            dve.wait_ge(g_final_in, 16)
            for n in range(2 * TT):
                t, c = n // 2, slice((n % 2) * (D // 2), (n % 2 + 1) * (D // 2))
                dve.scalar_tensor_tensor(out=normed[:, t, c], in0=x_tok[:, t, c], scalar=rstd[:, t:t + 1],
                                         in1=g_final_sb[:, c], op0=ALU.mult, op1=ALU.mult).then_inc(out_made, 1)


_INS = ["x", "positions", "g_mix", "w_in", "w_gate", "lambda_params", "g_subln", "w_br_diff",
        "w_br_sb", "w_out", "g_moe", "w_group", "b_group", "w_router", "b_router", "w_up_gate",
        "w_up", "w_down", "g_final"]


def kernel(**inputs):
    import numpy as _np
    import concourse.bacc as _bacc
    from concourse import mybir as _mybir
    from concourse.bass_utils import run_bass_kernel_spmd as _run

    nc = _bacc.Bacc("TRN2", target_bir_lowering=False, num_devices=1)
    arrays, args = {}, []
    for name in _INS:
        a = _np.ascontiguousarray(inputs[name])
        arrays[f"in_{name}"] = a
        args.append(nc.dram_tensor(f"in_{name}", a.shape, _mybir.dt.from_np(a.dtype), kind="ExternalInput").ap())
    out = nc.dram_tensor("block_out", inputs["x"].shape, _mybir.dt.float32, kind="ExternalOutput").ap()
    decoder_block(nc, *args, out)
    r = _run(nc, [arrays], core_ids=[0])
    return r.results[0]["block_out"]
```

```python
from contextlib import ExitStack

import numpy as np

import concourse.bass as bass
from concourse import mybir
from concourse.alu_op_type import AluOpType as ALU

F32 = mybir.dt.float32
I32 = mybir.dt.int32
BF16 = mybir.dt.bfloat16
ACT = mybir.ActivationFunctionType
AX = mybir.AxisListType.X

P = 128
BLK = 512
ROPE_THETA = 500000.0
EPS = 1e-6
LAMBDA_INIT = 0.8 - 0.6 * float(np.exp(-0.3 * 0))
BIG = 1e30
RING = 4
MORE = 4
SLOTS = 32
SIDE = 4
TWO_PI = (6.28125, 0.0019350051879882812, 3.0199159819e-07)
ROUND = float(3 << 22)
TYPES = 6
DQ, DK, DV, SQ, SK, SV = range(TYPES)


def decoder_block(nc, x, positions, g_mix, w_in, w_gate, lambda_params, g_subln, w_br_diff,
                  w_br_sb, w_out, g_moe, w_group, b_group, w_router, b_router, w_up_gate, w_up,
                  w_down, g_final, out):
    _, T, D = x.shape
    TT = T // P
    KD = D // P
    HV = g_subln.shape[1]
    HQ = lambda_params.shape[2]
    HEADS = w_br_diff.shape[1] // HV
    HALF = HQ // 4 // 2
    NG = w_group.shape[2]
    NE = w_router.shape[2]
    PER = NE // NG
    FF = w_up.shape[3]
    IN_BLOCKS = w_in.shape[2] // BLK
    GATE_BLOCKS = w_gate.shape[2] // BLK
    OUT_BLOCKS = D // BLK
    assert TT == 2 and HV == P and 2 * HQ == P and w_in.shape[2] == TYPES * HEADS * P
    assert GATE_BLOCKS == HEADS and FF == BLK and OUT_BLOCKS == 4 and KD == 16
    KH = KD // 2
    PAIR = 2
    GROUPS = NE // SIDE
    MAX_PASSES = T // SLOTS
    TURN_GATE = IN_BLOCKS // PAIR
    TURN_BR = TURN_GATE + GATE_BLOCKS // PAIR
    TURN_OUT = TURN_BR + 2 * OUT_BLOCKS // RING
    TURN_MOE = TURN_OUT + 2 * OUT_BLOCKS // RING
    USED_MOE = RING * TURN_MOE
    LOADS = KD + 2 * (FF // P)
    MOE_RING = RING + MORE
    MOE_TURNS = LOADS // MOE_RING
    assert LOADS % MOE_RING == 0

    ctx = ExitStack()
    with ctx:
        def sb(name, shape, dt=F32):
            return ctx.enter_context(nc.sbuf_tensor(name, shape, dt))

        def sem(name):
            return ctx.enter_context(nc.semaphore(name))

        ring = sb("ring", [P, RING, KH * BLK])
        x_tok = sb("x_tok", [P, TT, D])
        hT = sb("hT", [P, KD, T])
        qkv = sb("qkv", [P, TT, TYPES, HEADS, P])
        gates = sb("gates", [P, TT, 2 * D])
        small_mem = sb("small_mem", [P, 5120])

        def part(flat, at, *shape):
            n = int(np.prod(shape))
            v = flat[:, at:at + n]
            if len(shape) == 2:
                return v.rearrange("p (a b) -> p a b", a=shape[0])
            if len(shape) == 3:
                return v.rearrange("p (a b c) -> p a b c", a=shape[0], b=shape[1])
            return v

        SLOT = KH * BLK
        qkv_flat = qkv[:, :, :, :, :].rearrange("p a b c d -> p (a b c d)")
        normed = part(qkv_flat, 0, TT, D)
        mixT = part(qkv_flat, 0, KD, T)
        junk = part(qkv_flat, SLOT, D)
        gates_flat = gates[:, :, :].rearrange("p a b -> p (a b)")
        rope_tmp = part(gates_flat, 0, 4, 2 * 2 * HEADS, HALF)
        slots = [ring[:, s] for s in range(RING)] + [part(qkv_flat, (1 + s) * SLOT, SLOT) for s in range(2)] \
            + [part(gates_flat, s * SLOT, SLOT) for s in range(2)]
        hT_flat = hT[:, :, :].rearrange("p a b -> p (a b)")
        xgT = part(hT_flat, 0, KD, P)
        y_sb = part(hT_flat, KD * P, D)
        stage = part(small_mem, 0, TT, 4, P)
        qkT = part(small_mem, 1024, 4, T)
        prob = part(small_mem, 2048, 2, 3 * P)
        diff, z, soft, stick, aT_diff, aT_sb = (part(small_mem, 2816 + n * 3 * P, 3 * P) for n in range(6))
        act_sb = part(small_mem, 0, 2, BLK)
        squares = part(small_mem, 0, BLK)
        actT = part(small_mem, 1024, FF // P, P)
        pick = part(small_mem, 1536, 2, TT, P)
        placeT = part(small_mem, 2048, T)
        g_final_sb = part(small_mem, 2304, D)
        routing = part(small_mem, 4352, 768)
        at = [0]

        def small(*shape):
            v = part(routing, at[0], *shape)
            at[0] += int(np.prod(shape))
            return v

        logits = small(TT, NG + NE)
        best = small(TT, 1)
        best8 = small(TT, 8)
        best_at = small(TT, 2)
        shifted = small(TT, NG + 1)
        is_group = small(TT, NG)
        masked = small(TT, NE)
        is_top = [small(TT, NE), small(TT, NE)]
        tie = small(TT, NG)
        tie_top = small(TT, 1)
        chosen = small(TT, NE)
        combine = small(TT, NE)
        rank = small(TT, NE)
        pair_w = small(TT, 4)
        over = small(MAX_PASSES - 1)
        count = small(2)

        ident = sb("ident", [P, P])
        before = sb("before", [P, P])
        ones = sb("ones", [P, P])
        before_b = sb("before_b", [P, P], BF16)
        ones_b = sb("ones_b", [P, P], BF16)
        chosen_b = sb("chosen_b", [P, TT, NE], BF16)
        mask_upto = sb("mask_upto", [P, 3 * P])
        mask_before = sb("mask_before", [P, 3 * P])
        gsub = sb("gsub", [P, HV])
        slot_id = sb("slot_id", [P, SLOTS])
        falling = sb("falling", [P, NG])
        expert_id = sb("expert_id", [P, NE])
        starts = sb("starts", [P, MAX_PASSES - 1])
        inv_freq = sb("inv_freq", [P, HALF])
        g_mix_sb = sb("g_mix_sb", [P, KD])
        g_moe_sb = sb("g_moe_sb", [P, KD])
        w_route = sb("w_route", [P, KD, NG + NE])
        b_route = sb("b_route", [P, NG + NE])
        lam_sb = sb("lam_sb", [P, 4, HQ])
        pos_i = sb("pos_i", [P, TT], I32)
        passes_i = sb("passes_i", [P, 1], I32)
        place8 = sb("place8", [P, TT, 8], mybir.dt.uint32)
        pos_f = sb("pos_f", [P, TT])
        angle = sb("angle", [P, TT, HALF])
        whole = sb("whole", [P, TT, HALF])
        sin = sb("sin", [P, TT, HALF])
        cos = sb("cos", [P, TT, HALF])
        lam_two = sb("lam_two", [P, 2])
        neg_lam = sb("neg_lam", [P, 1])
        top = sb("top", [P, TT, 2])
        neg_top = sb("neg_top", [P, TT, 2])
        total = sb("total", [P, TT, 2])
        weight = sb("weight", [P, TT, 2])
        ssq = sb("ssq", [P, TT, OUT_BLOCKS])
        var = sb("var", [P, TT])
        rstd_in = sb("rstd_in", [P, TT])
        rstd = sb("rstd", [P, TT])
        newton = sb("newton", [P, TT])

        bank = [ctx.enter_context(nc.psum_tensor(f"bank{i}", [P, BLK], F32)) for i in range(8)]

        x_in = [sem(f"x_in{t}") for t in range(TT)]
        g_mix_in = sem("g_mix_in")
        early_in = sem("early_in")
        route_in = sem("route_in")
        g_final_in = sem("g_final_in")
        out_written = sem("out_written")
        slot_full = [sem(f"slot_full{i}") for i in range(RING + MORE)]
        slots_used = sem("slots_used")
        masks_made = sem("masks_made")
        rope_made = sem("rope_made")
        sines_made = sem("sines_made")
        angles_made = sem("angles_made")
        lam_summed = sem("lam_summed")
        lam_exped = sem("lam_exped")
        squared = sem("squared")
        rstd_made = sem("rstd_made")
        round_squared = sem("round_squared")
        normed_made = sem("normed_made")
        x_turned = sem("x_turned")
        xT_made = sem("xT_made")
        turned = sem("turned")
        turned_act = sem("turned_act")
        turned_dve = sem("turned_dve")
        proj_act = sem("proj_act")
        proj_dve = sem("proj_dve")
        staged = sem("staged")
        qk_turned = sem("qk_turned")
        qkT_act = sem("qkT_act")
        qkT_dve = sem("qkT_dve")
        diff_scored = sem("diff_scored")
        sb_scored = sem("sb_scored")
        tops_made = sem("tops_made")
        z_made = sem("z_made")
        diff_exped = sem("diff_exped")
        soft_made = sem("soft_made")
        stick_summed = sem("stick_summed")
        stick_exped = sem("stick_exped")
        diff_made = sem("diff_made")
        diff_turned = sem("diff_turned")
        sb_turned = sem("sb_turned")
        aT_act = sem("aT_act")
        aT_dve = sem("aT_dve")
        heads_out = sem("heads_out")
        head_squared = sem("head_squared")
        heads_stored = sem("heads_stored")
        gates_open = sem("gates_open")
        mixed = sem("mixed")
        mix_turned = sem("mix_turned")
        mixT_made = sem("mixT_made")
        x_added = sem("x_added")
        logits_made = sem("logits_made")
        route_shifted = sem("route_shifted")
        route_exped = sem("route_exped")
        first_weighed = sem("first_weighed")
        combine_made = sem("combine_made")
        chosen_made = sem("chosen_made")
        ranks_made = sem("ranks_made")
        passes_made = sem("passes_made")
        count_made = sem("count_made")
        picks_made = sem("picks_made")
        places_made = sem("places_made")
        gathered = sem("gathered")
        xg_made = sem("xg_made")
        place_turned = sem("place_turned")
        placeT_made = sem("placeT_made")
        silu_made = sem("silu_made")
        act_made = sem("act_made")
        act_turned = sem("act_turned")
        actT_made = sem("actT_made")
        y_act = sem("y_act")
        y_dve = sem("y_dve")
        combined = sem("combined")
        added = sem("added")
        out_made = sem("out_made")

        x_d = x[0].rearrange("(t p) d -> t p d", p=P)
        out_d = out[0].rearrange("(t p) d -> t p d", p=P)
        w_in_d = w_in[0].rearrange("(h q k p) (b n) -> h q b p k n", h=2, q=2, p=P, n=BLK)
        w_gate_d = w_gate[0].rearrange("(h q k p) (b n) -> h q b p k n", h=2, q=2, p=P, n=BLK)
        w_out_d = w_out[0].rearrange("(h q k p) (b n) -> h q b p k n", h=2, q=2, p=P, n=BLK)
        w_br_d = [w[0].rearrange("(q k p) (b n) -> q b p k n", q=2, p=P, n=BLK)
                  for w in (w_br_diff, w_br_sb)]
        up_d = [w[0].rearrange("(g e) (k p) n -> k g p e n", e=SIDE, p=P) for w in (w_up_gate, w_up)]
        down_d = w_down[0].rearrange("(g e) (f u p) (b n) -> b f u g p e n", e=SIDE, u=2, p=P, n=BLK)

        def slot(s):
            return slots[s].rearrange("p (k n) -> p k n", n=BLK)

        qkv_cols = qkv[:, :, :, :, :].rearrange("p t a (c h) d -> p t (a c) (h d)", c=2)
        gate_cols = gates[:, :, :].rearrange("p t (b n) -> p t b n", n=BLK)
        x_cols = x_tok[:, :, :].rearrange("p t (b n) -> p t b n", n=BLK)

        def vec(a):
            return a.rearrange("a (k p) -> p (a k)", p=P)

        block = ctx.enter_context(nc.Block())

        @block.sync
        def _(sp):
            sp.sem_inc(slots_used, RING)
            for t in range(TT):
                sp.dma_start(x_tok[:, t], x_d[t]).then_inc(x_in[t], 16)

            def fill(s, quarters):
                for q, src in reversed(list(enumerate(quarters))):
                    dst = slots[s][:, q * 4 * BLK:(q + 1) * 4 * BLK]
                    dst = dst.rearrange("p (k n) -> p k n", k=src.shape[1])
                    sp.dma_start(dst, src).then_inc(slot_full[s], 16)

            def load(s, turn, quarters):
                sp.wait_ge(slots_used, RING * turn + s + 1)
                fill(s, quarters)

            def expert_quarters(n, g, ahead=0):
                if n < KD:
                    return [w[n, ahead:][g] for w in up_d]
                n -= KD
                return [down_d[n // 2, n % 2, u, ahead:][g] for u in range(2)]

            def load_experts(g, m, loads, ahead=0):
                for n in loads:
                    sp.wait_ge(slots_used, m * LOADS + (USED_MOE + RING + n - MOE_RING + 1 + ahead * LOADS))
                    fill((n + RING) % MOE_RING, expert_quarters(n, g, ahead))

            with sp.Fori(0, TURN_GATE) as i:
                for s in range(RING):
                    load(s, i, [w_in_d[s % 2, q].rearrange("(i j) p k n -> i j p k n", j=PAIR)[i, s // 2]
                                for q in range(2)])
            with sp.Fori(0, GATE_BLOCKS // PAIR) as i:
                for s in range(RING):
                    load(s, i + TURN_GATE, [w_gate_d[s % 2, q].rearrange("(i j) p k n -> i j p k n", j=PAIR)[i, s // 2]
                                            for q in range(2)])
            for n in range(2 * OUT_BLOCKS):
                load(n % RING, TURN_BR + n // RING, [w_br_d[n % 2][q, n // 2] for q in range(2)])
            sp.wait_ge(turned, KH)
            for n in (0, 1):
                fill(RING + n, expert_quarters(n, 0))
            for n in range(2 * OUT_BLOCKS):
                if n == RING:
                    sp.wait_ge(mix_turned, 2 * OUT_BLOCKS)
                    for k in (2, 3):
                        fill(RING + k, expert_quarters(k, 0))
                load(n % RING, TURN_OUT + n // RING, [w_out_d[n % 2, q, n // 2] for q in range(2)])
            with sp.Fori(0, GROUPS - 1) as g:
                load_experts(g, g, range(MORE, LOADS))
                load_experts(g, g, range(MORE), ahead=1)
            load_experts(GROUPS - 1, GROUPS - 1, range(MORE, LOADS))
            sp.wait_ge(passes_made, 1)
            passes = sp.value_load(passes_i[0:1, 0:1], min_val=1, max_val=MAX_PASSES)
            with sp.If(passes > 1):
                with sp.Fori(1, passes) as again:
                    with sp.Fori(0, GROUPS) as g:
                        load_experts(g, again * GROUPS + g, range(LOADS))
            for n in range(OUT_BLOCKS * TT):
                t, c = n // OUT_BLOCKS, slice(n % OUT_BLOCKS * BLK, (n % OUT_BLOCKS + 1) * BLK)
                sp.wait_ge(out_made, n + 1)
                sp.dma_start(out_d[t][:, c], normed[:, t, c]).then_inc(out_written, 16)
            sp.wait_ge(out_written, 16 * OUT_BLOCKS * TT)

        @block.gpsimd
        def _(pool):
            pool.sem_inc(qk_turned, 1)
            pool.memset(ident[:], 0.0)
            pool.memset(ones[:], 1.0)
            pool.memset(mask_upto[:], 0.0)
            pool.memset(mask_before[:], 0.0)
            for i in range(HALF):
                f = np.float32(ROPE_THETA) ** np.float32(-2.0 * i / (2 * HALF))
                pool.memset(inv_freq[:, i:i + 1], float(f))
            pool.iota(slot_id[:], [[1, SLOTS]], base=0, channel_multiplier=0,
                      allow_small_or_imprecise_dtypes=True)
            pool.iota(expert_id[:], [[1, NE]], base=0, channel_multiplier=0,
                      allow_small_or_imprecise_dtypes=True)
            pool.iota(falling[:], [[-1, NG]], base=NG, channel_multiplier=0,
                      allow_small_or_imprecise_dtypes=True)
            pool.iota(starts[:], [[SLOTS, MAX_PASSES - 1]], base=SLOTS, channel_multiplier=0,
                      allow_small_or_imprecise_dtypes=True)
            pool.drain()
            pool.affine_select(out=ident[:], in_=ident[:], compare_op=ALU.not_equal, fill=1.0,
                               base=0, pattern=[[-1, P]], channel_multiplier=1)
            pool.affine_select(out=before[:], in_=ones[:], compare_op=ALU.is_ge, fill=0.0,
                               base=-1, pattern=[[1, P]], channel_multiplier=-1)
            for m, off in ((mask_upto, 0), (mask_before, -1)):
                for c in (0, 2 * P):
                    pool.affine_select(out=m[:, c:c + P], in_=m[:, c:c + P], compare_op=ALU.is_ge,
                                       fill=-BIG, base=off, pattern=[[-1, P]], channel_multiplier=1)
            pool.tensor_copy(ones_b[:], ones[:])
            pool.drain()
            pool.tensor_copy(before_b[:], before[:])
            pool.drain().then_inc(masks_made, 1)
            with nc.allow_non_contiguous_dma("small vectors"):
                pool.dma_start(g_moe_sb[:], vec(g_moe)).then_inc(route_in, 16)
                pool.dma_start(w_route[:, :, 0:NG], w_group[0].rearrange("(k p) n -> p k n", p=P)).then_inc(route_in, 16)
                pool.dma_start(w_route[:, :, NG:], w_router[0].rearrange("(k p) n -> p k n", p=P)).then_inc(route_in, 16)
                pool.dma_start(b_route[:, 0:NG], b_group[0].partition_broadcast(P)).then_inc(route_in, 16)
                pool.dma_start(b_route[:, NG:], b_router[0].partition_broadcast(P)).then_inc(route_in, 16)

            rope_blocks = 2 * HEADS * P // BLK
            pool.wait_ge(sines_made, 2)
            pool.wait_ge(proj_act, 2 + rope_blocks)
            pool.wait_ge(proj_dve, 2 + rope_blocks)
            for t in range(TT):
                qk = qkv[:, t, DQ:DK + 1, :, :].rearrange("p a h (c d) -> p (a h c) d", c=2)
                first, second = qk[:, :, 0:HALF], qk[:, :, HALF:2 * HALF]
                c = cos[:, t].unsqueeze(1).broadcast_to([P, 4 * HEADS, HALF])
                s = sin[:, t].unsqueeze(1).broadcast_to([P, 4 * HEADS, HALF])
                if t:
                    pool.drain()
                pool.tensor_tensor(rope_tmp[:, 0], first, c, ALU.mult)
                pool.tensor_tensor(rope_tmp[:, 1], second, s, ALU.mult)
                pool.tensor_tensor(rope_tmp[:, 2], second, c, ALU.mult)
                pool.tensor_tensor(rope_tmp[:, 3], first, s, ALU.mult)
                pool.drain()
                pool.tensor_tensor(first, rope_tmp[:, 0], rope_tmp[:, 1], ALU.subtract)
                pool.tensor_tensor(second, rope_tmp[:, 2], rope_tmp[:, 3], ALU.add)
            pool.drain()
            pool.wait_ge(proj_act, 2 + SV * HEADS * P // BLK)
            pool.wait_ge(proj_dve, 2 + SV * HEADS * P // BLK)

            def stage_head(head):
                pool.wait_ge(qk_turned, head + 1)
                for n, a in enumerate((DQ, DK, SQ, SK)):
                    pool.tensor_copy(stage[:, :, n], qkv[:, :, a].rearrange("p t h d -> p h t d")[:, head])
                pool.drain().then_inc(staged, 1)

            with pool.Fori(0, HEADS) as head:
                stage_head(head)

            pool.wait_ge(x_added, TT * OUT_BLOCKS)
            pool.dma_start(g_final_sb, g_final.partition_broadcast(P)).then_inc(g_final_in, 16)

            pool.wait_ge(first_weighed, 1)
            pool.tensor_tensor(pair_w[:, :, 3:4], pair_w[:, :, 2:3], shifted[:, :, NG:NG + 1], ALU.mult)
            pool.drain()
            for c in range(2):
                pool.tensor_tensor(is_top[c], is_top[c], pair_w[:, :, 2 + c:3 + c].broadcast_to([P, TT, NE]),
                                   ALU.mult)
            pool.drain()
            pool.tensor_tensor(combine, is_top[0], is_top[1], ALU.add).then_inc(combine_made, 1)

            pool.wait_ge(count_made, 1)
            pool.tensor_scalar(over, starts[:], count[:, 0:1], None, ALU.is_lt)
            pool.drain()
            pool.tensor_scalar(count[:, 1:2], over[:, 0:1], 1.0, None, ALU.add)
            for n in range(1, MAX_PASSES - 1):
                pool.drain()
                pool.tensor_tensor(count[:, 1:2], count[:, 1:2], over[:, n:n + 1], ALU.add)
            pool.drain()
            pool.tensor_copy(passes_i[:], count[:, 1:2])
            pool.drain().then_inc(passes_made, 1)

        @block.tensor
        def _(pe):
            def turn_heads():
                for m in range(KH):
                    if m >= 4:
                        pe.wait_ge((turned_act, turned_dve)[m % 2], 2 * ((m - 4) // 2 + 1))
                    elif m == 3:
                        pe.wait_ge(heads_stored, HEADS + 1)
                    for k in range(2):
                        a, head = (DQ, SQ)[(2 * m + k) // HEADS], (2 * m + k) % HEADS
                        for t in range(TT):
                            c = k * T + t * P
                            mm = pe.transpose(bank[4 + m % 4][:, c:c + P], qkv[:, t, a, head], ident[:])
                    mm.then_inc(turned, 1)

            def turn_x2(n):
                pe.wait_ge(x_added, TT * (n + 1))
                for c in range(2):
                    pe.wait_ge((turned_act, turned_dve)[c], KH + 2 * n)
                    for k in range(2):
                        for t in range(TT):
                            at = (2 * c + k) * P
                            mm = pe.transpose(bank[4 + c][:, k * T + t * P:k * T + (t + 1) * P],
                                              x_cols[:, t, n, at:at + P], ident[:])
                    mm.then_inc(turned, 1)

            def route_block(n):
                last = n == OUT_BLOCKS - 1
                pe.wait_ge(turned_act, KH + 2 * (n + 1))
                if not last:
                    pe.wait_ge(turned_dve, KH + 2 * (n + 1))
                for k in range(4 * n, 4 * n + 4):
                    if last and k % 4 == 2:
                        pe.wait_ge(turned_act, KH + 2 * (n + 2))
                    for t in range(TT):
                        mm = pe.matmul(bank[6 + t][:, 0:NG + NE], hT[:, k, t * P:(t + 1) * P],
                                       w_route[:, k], start=(k == 0), stop=(k == KD - 1))
                return mm

            def project(n, j, turn, quarters):
                for half in range(2):
                    s = 2 * j + half
                    for q in range(2):
                        if half == 0 and q == 0:
                            pe.wait_ge(proj_act, n + 1)
                            pe.wait_ge(proj_dve, n + 1)
                        if q == 0:
                            pe.wait_ge(slot_full[s], 32 * (turn + 1))
                        for k in range(4 * q, 4 * q + 4):
                            for t in range(TT):
                                mm = pe.matmul(bank[2 * j + t][:], hT[:, KH * half + k, t * P:(t + 1) * P],
                                               slot(s)[:, k], start=(half == 0 and k == 0),
                                               stop=(half == 1 and k == KH - 1))
                        if q == 1:
                            mm.then_inc(slots_used, 1)
                        quarters(2 * half + q)

            pe.wait_ge(masks_made, 1)
            for t in range(TT):
                pe.wait_ge(x_in[t], 16)
                for m in range(4):
                    for k in range(4):
                        mm = pe.transpose(bank[4 * t + m][:, k * P:(k + 1) * P],
                                          x_tok[:, t, (4 * m + k) * P:(4 * m + k + 1) * P], ident[:])
                    mm.then_inc(x_turned, 1)
            pe.wait_ge(xT_made, 4 * TT)
            with pe.Fori(0, TURN_GATE) as i:
                for j in range(PAIR):
                    project(i * PAIR + j, j, i, lambda q: None)

            def attend(head, step):
                if step == 0:
                    pe.wait_ge(qkT_act, head + 1)
                    pe.wait_ge(qkT_dve, head + 1)
                    pe.wait_ge(heads_stored, head + 1)
                    for t in range(TT):
                        for m in range(2):
                            r, c = slice(m * HQ, (m + 1) * HQ), slice(t * P, (2 * t + 1) * P)
                            mm = pe.matmul(bank[6 + m][:, c], qkT[r, 0, t * P:(t + 1) * P],
                                           qkT[r, 1, 0:(t + 1) * P], start=True, stop=True)
                    mm.then_inc(diff_scored, 1)
                    pe.matmul(bank[4][:, 0:P], qkT[:, 2, 0:P], qkT[:, 3, 0:P], start=True, stop=True)
                    pe.matmul(bank[4][:, P:3 * P], qkT[:, 2, P:T], qkT[:, 3, :],
                              start=True, stop=True).then_inc(sb_scored, 1)
                if step == 2:
                    pe.wait_ge(diff_made, head + 1)
                    for c in range(3):
                        mm = pe.transpose(bank[5][:, c * P:(c + 1) * P], diff[:, c * P:(c + 1) * P], ident[:])
                    mm.then_inc(diff_turned, 1)
                    pe.wait_ge(stick_exped, head + 1)
                    for c in range(3):
                        mm = pe.transpose(bank[6][:, c * P:(c + 1) * P], stick[:, c * P:(c + 1) * P], ident[:])
                    mm.then_inc(sb_turned, 1)
                if step == 3:
                    pe.wait_ge(aT_act, head + 1)
                    pe.wait_ge(aT_dve, head + 1)
                    for n, (aT, a) in enumerate(((aT_diff, DV), (aT_sb, SV))):
                        v = [qkv[:, t, a][:, head] for t in range(TT)]
                        o = bank[7][:, n * T:(n + 1) * T]
                        pe.matmul(o[:, 0:P], aT[:, 0:P], v[0], start=True, stop=True)
                        pe.matmul(o[:, P:T], aT[:, P:2 * P], v[0], start=True, stop=False)
                        mm = pe.matmul(o[:, P:T], aT[:, 2 * P:3 * P], v[1], start=False, stop=True)
                    mm.then_inc(heads_out, 1)

            with pe.Fori(0, GATE_BLOCKS // PAIR) as i:
                for j in range(PAIR):
                    head = i * PAIR + j
                    pe.wait_ge(staged, head + 1)
                    for n in range(4):
                        for t in range(TT):
                            c = (n % 2) * T + t * P
                            mm = pe.transpose(bank[4 + n // 2][:, c:c + P], stage[:, t, n], ident[:])
                    mm.then_inc(qk_turned, 1)
                    project(head + IN_BLOCKS, j, i + TURN_GATE, lambda q: attend(head, q))

            pe.wait_ge(heads_stored, HEADS)
            turn_heads()
            pe.wait_ge(proj_act, 2 + IN_BLOCKS + GATE_BLOCKS)
            pe.wait_ge(proj_dve, 2 + IN_BLOCKS + GATE_BLOCKS)

            def turn_mixed(n):
                pe.wait_ge(mixed, 2 * n + 2)
                for c in range(2):
                    if n:
                        pe.wait_ge(mixT_made, 2 * n + c - 1)
                    for k in range(2):
                        for t in range(TT):
                            at = (2 * c + k) * P
                            mm = pe.transpose(bank[6 + c][:, k * T + t * P:k * T + (t + 1) * P],
                                              gate_cols[:, t, n, at:at + P], ident[:])
                    mm.then_inc(mix_turned, 1)

            for n in range(2 * OUT_BLOCKS):
                pair = 2 * (n % 3)
                if n < 2:
                    pe.wait_ge(turned_act, KH // 2 * (n + 1))
                    pe.wait_ge(turned_dve, KH // 2 * (n + 1))
                if n >= 3:
                    pe.wait_ge(mixed, n - 2)
                pe.wait_ge(slot_full[n % RING], 32 * (TURN_BR + n // RING + 1))
                for k in range(KH):
                    for t in range(TT):
                        mm = pe.matmul(bank[pair + t][:], hT[:, KH * (n % 2) + k, t * P:(t + 1) * P],
                                       slot(n % RING)[:, k], start=(k == 0), stop=(k == KH - 1))
                mm.then_inc(slots_used, 1)
                if n % 2 and n > 1:
                    turn_mixed(n // 2 - 1)
            turn_mixed(OUT_BLOCKS - 1)
            pe.wait_ge(mixT_made, 2 * OUT_BLOCKS)
            for n in range(OUT_BLOCKS):
                pair = 2 * (n % 2)
                if n >= 2:
                    pe.wait_ge(x_added, TT * (n - 1))
                for half in range(2):
                    m = 2 * n + half
                    pe.wait_ge(slot_full[m % RING], 32 * (TURN_OUT + m // RING + 1))
                    for k in range(KH):
                        for t in range(TT):
                            mm = pe.matmul(bank[pair + t][:], mixT[:, KH * half + k, t * P:(t + 1) * P],
                                           slot(m % RING)[:, k], start=(half == 0 and k == 0),
                                           stop=(half == 1 and k == KH - 1))
                    mm.then_inc(slots_used, 1)
                    if n and half == 0:
                        turn_x2(n - 1)
                    if n == 1 and half == 0:
                        pe.wait_ge(route_in, 16 * 5)
                    if 0 < n < OUT_BLOCKS - 1 and half == 1:
                        route_block(n - 1)
            route_block(OUT_BLOCKS - 2)
            turn_x2(OUT_BLOCKS - 1)
            route_block(OUT_BLOCKS - 1).then_inc(logits_made, 1)
            pe.wait_ge(chosen_made, 1)
            for t in range(TT):
                for u in range(t + 1):
                    pe.matmul(bank[1][:, t * NE:(t + 1) * NE], (before_b if u == t else ones_b)[:],
                              chosen_b[:, u], start=(u == 0), stop=(u == t))
            for u in range(TT):
                mm = pe.matmul(bank[1][:, TT * NE:(TT + 1) * NE], ones_b[:], chosen_b[:, u],
                               start=(u == 0), stop=(u == TT - 1))
            mm.then_inc(ranks_made, 1)

            def experts(m):
                def wait_slot(n):
                    s = (n + RING) % MOE_RING
                    pe.wait_ge(slot_full[s], (m * MOE_TURNS + (n // MOE_RING + 1 + (TURN_MOE if s < RING else 0))) * 32)
                    return slot(s)

                def combine_block(b):
                    pe.wait_ge((y_dve, y_act)[b % 2], m * (OUT_BLOCKS // 2) + b // 2 + 1)
                    for t in range(TT):
                        n = TT * b + t
                        if n >= 4:
                            pe.wait_ge(added, m * (4 * TT) + (n - 2))
                        pe.matmul(bank[(2 + n) % 4][:], placeT[:, t * P:(t + 1) * P],
                                  y_sb[:, b * BLK:(b + 1) * BLK], start=True, stop=True).then_inc(combined, 1)

                def gather(q):
                    if q % 2 == 0:
                        pe.wait_ge(normed_made, TT * (q // 2 + 1))
                    if q >= 2:
                        pe.wait_ge(xg_made, m * KH + q - 1)
                    for k in range(2):
                        for t in range(TT):
                            mm = pe.matmul(bank[2 + q % 2][:, k * P:(k + 1) * P],
                                           normed[:, t, (2 * q + k) * P:(2 * q + k + 1) * P],
                                           pick[:, 0, t], start=(t == 0), stop=(t == TT - 1))
                    mm.then_inc(gathered, 1)

                pe.wait_ge(picks_made, m + 1)
                pe.wait_ge(added, m * 2 * TT * 2 + 1)
                gather(0)
                for k in range(KD):
                    if k % 2 and k < KD - 1:
                        gather(k // 2 + 1)
                    if k == 12:
                        pe.wait_ge(places_made, m + 1)
                        for t in range(TT):
                            mm = pe.transpose(bank[5][:, t * P:(t + 1) * P], pick[:, 1, t], ident[:])
                        mm.then_inc(place_turned, 1)
                    if k % 2 == 0:
                        pe.wait_ge(xg_made, m * KH + k // 2 + 1)
                    weights = wait_slot(k)
                    for w in range(2):
                        for j in range(SIDE):
                            c = slice(j * SLOTS, (j + 1) * SLOTS)
                            mm = pe.matmul(bank[w][c, :], xgT[:, k, c], weights[:, 4 * w + j],
                                           start=(k == 0), stop=(k == KD - 1),
                                           tile_position=(0, j * SLOTS))
                    mm.then_inc(slots_used, 1)
                pe.wait_ge(act_made, m + 1)
                for f in range(FF // P):
                    mm = pe.transpose(bank[4][:, f * P:(f + 1) * P], act_sb[:, 1, f * P:(f + 1) * P], ident[:])
                mm.then_inc(act_turned, 1)
                pe.wait_ge(actT_made, m + 1)
                pe.wait_ge(placeT_made, m + 1)
                for n in range(2 * OUT_BLOCKS):
                    b = n // 2
                    weights = wait_slot(KD + n)
                    for u in range(2):
                        f = 2 * (n % 2) + u
                        for j in range(SIDE):
                            c = slice(j * SLOTS, (j + 1) * SLOTS)
                            mm = pe.matmul(bank[4 + b][c, :], actT[:, f, c], weights[:, SIDE * u + j],
                                           start=(f == 0), stop=(f == FF // P - 1),
                                           tile_position=(0, j * SLOTS))
                    mm.then_inc(slots_used, 1)
                    if b and n % 2 == 0:
                        combine_block(b - 1)
                combine_block(OUT_BLOCKS - 1)

            with pe.Fori(0, GROUPS) as g:
                experts(g)
            pe.wait_ge(passes_made, 1)
            passes = pe.value_load(passes_i[0:1, 0:1], min_val=1, max_val=MAX_PASSES)
            with pe.If(passes > 1):
                with pe.Fori(1, passes) as again:
                    with pe.Fori(0, GROUPS) as g:
                        experts(again * GROUPS + g)

        @block.scalar
        def _(act):
            act.sem_inc(proj_act, 2)
            with nc.allow_non_contiguous_dma("small vectors"):
                act.dma_start(g_mix_sb[:], vec(g_mix)).then_inc(g_mix_in, 16)
                act.dma_start(lam_sb[:], lambda_params[0].partition_broadcast(P)).then_inc(early_in, 16)
                act.dma_start(gsub[:], g_subln[0].partition_broadcast(P)).then_inc(early_in, 16)
                act.dma_start(pos_i[:], positions.rearrange("a (t p) -> p (a t)", p=P)).then_inc(early_in, 16)

            for t in range(TT):
                act.wait_ge(x_in[t], 16)
                if t:
                    act.drain()
                act.activation(junk, x_tok[:, t], ACT.Square, accum_out=ssq[:, t, 0:1])
            act.drain().then_inc(squared, 1)
            act.wait_ge(lam_summed, 1)
            act.activation(lam_two[:], lam_two[:], ACT.Exp).then_inc(lam_exped, 1)
            act.wait_ge(angles_made, 1)
            act.activation(sin[:], angle[:], ACT.Sin).then_inc(sines_made, 1)
            act.activation(cos[:], angle[:], ACT.Sin, scale=0.5).then_inc(angles_made, 1)

            def copy_block(n, j, dst):
                act.wait_ge(slots_used, (n + 1) * 2 + RING)
                act.activation(dst, bank[2 * j][:], ACT.Copy, scale=rstd_in[:, 0:1]).then_inc(proj_act, 1)

            act.wait_ge(rstd_made, 1)
            with act.Fori(0, TURN_GATE) as i:
                for j in range(PAIR):
                    dst = qkv_cols[:, 0].rearrange("p (i j) n -> p i j n", j=PAIR)[:, i, j]
                    copy_block(i * PAIR + j, j, dst)

            with act.Fori(0, GATE_BLOCKS // PAIR) as i:
                for j in range(PAIR):
                    head = i * PAIR + j
                    act.wait_ge(qk_turned, head + 2)
                    act.activation(qkT[:, 0:2], bank[4][:], ACT.Copy).then_inc(qkT_act, 1)
                    act.wait_ge(tops_made, head + 1)
                    for t in range(TT):
                        for m in range(2):
                            p_ = prob[:, m, 0:P] if t == 0 else prob[:, m, P:3 * P]
                            act.activation(p_, p_, ACT.Exp, bias=neg_top[:, t, m:m + 1],
                                           accum_out=total[:, t, m:m + 1])
                    act.drain().then_inc(diff_exped, 1)
                    act.wait_ge(z_made, head + 1)
                    act.activation(soft[:], z[:], ACT.Abs)
                    act.drain()
                    act.activation(soft[:], soft[:], ACT.Exp, scale=-1.0)
                    act.drain()
                    act.activation(soft[:], soft[:], ACT.Ln, bias=1.0).then_inc(soft_made, 1)
                    act.wait_ge(stick_summed, head + 1)
                    act.activation(stick[:], stick[:], ACT.Exp).then_inc(stick_exped, 1)
                    act.wait_ge(diff_turned, head + 1)
                    act.activation(aT_diff[:], bank[5][:, 0:3 * P], ACT.Copy).then_inc(aT_act, 1)
                    act.wait_ge(heads_out, head + 1)
                    for t in range(TT):
                        act.activation(soft[:, t * P:(t + 1) * P], bank[7][:, t * P:(t + 1) * P],
                                       ACT.Square, accum_out=ssq[:, t, 0:1])
                    act.drain().then_inc(head_squared, 1)
                    copy_block(head + IN_BLOCKS, j,
                               gate_cols[:, 0].rearrange("p (i j) n -> p i j n", j=PAIR)[:, i, j])

            for m in range(0, KH, 2):
                act.wait_ge(turned, m + 1)
                for k in range(2):
                    act.activation(hT[:, 2 * m + k], bank[4 + m % 4][:, k * T:(k + 1) * T],
                                   ACT.Copy).then_inc(turned_act, 1)
            act.wait_ge(proj_dve, 2 + IN_BLOCKS + GATE_BLOCKS)
            for t in range(TT):
                act.activation(gates[:, t], gates[:, t], ACT.Sigmoid)
            act.drain().then_inc(gates_open, 1)
            for n in range(2 * OUT_BLOCKS):
                act.wait_ge(mix_turned, n + 1)
                act.activation(mixT[:, 2 * n:2 * n + 2].rearrange("p a b -> p (a b)"), bank[6 + n % 2][:],
                               ACT.Copy).then_inc(mixT_made, 1)
            act.wait_ge(route_in, 16 * 5)
            for n in range(OUT_BLOCKS):
                for t in range(TT):
                    act.wait_ge(x_added, TT * n + t + 1)
                    act.activation(squares, x_cols[:, t, n], ACT.Square, accum_out=ssq[:, t, n:n + 1])
                    act.drain()
                if n == OUT_BLOCKS - 1:
                    act.sem_inc(squared, 1)
                for c in range(2 if n == OUT_BLOCKS - 1 else 1):
                    act.wait_ge(turned, KH + 2 * n + c + 1)
                    for k in range(2):
                        at = 4 * n + 2 * c + k
                        act.activation(hT[:, at], bank[4 + c][:, k * T:(k + 1) * T], ACT.Copy,
                                       scale=g_moe_sb[:, at:at + 1]).then_inc(turned_act, 1)
            act.wait_ge(rstd_made, 2)
            for b in range(OUT_BLOCKS):
                if b == 2:
                    act.wait_ge(route_shifted, 1)
                    for t in range(TT):
                        act.activation(shifted[:, t, 0:NG], shifted[:, t, 0:NG], ACT.Exp,
                                       accum_out=pair_w[:, t, 0:1])
                    act.drain().then_inc(route_exped, 1)
                    act.wait_ge(route_shifted, 2)
                    act.activation(shifted[:, :, NG:NG + 1], shifted[:, :, NG:NG + 1],
                                   ACT.Exp).then_inc(route_exped, 1)
                for t in range(TT):
                    act.activation(normed[:, t, b * BLK:(b + 1) * BLK], x_cols[:, t, b], ACT.Copy,
                                   scale=rstd[:, t:t + 1]).then_inc(normed_made, 1)

            def experts(m):
                act.wait_ge(place_turned, m + 2)
                act.activation(placeT, bank[5][:, 0:T], ACT.Copy).then_inc(placeT_made, 1)
                act.wait_ge(slots_used, m * LOADS + (RING + USED_MOE + KD))
                act.activation(act_sb[:, 0], bank[0][:], ACT.Silu).then_inc(silu_made, 1)
                act.wait_ge(act_turned, m + 1)
                act.activation(actT.rearrange("p a b -> p (a b)"), bank[4][:], ACT.Copy).then_inc(actT_made, 1)
                for b in range(OUT_BLOCKS):
                    if b % 2:
                        act.wait_ge(slots_used, m * LOADS + (RING + USED_MOE + KD + 2 * (b + 1)))
                        act.activation(y_sb[:, b * BLK:(b + 1) * BLK], bank[4 + b][:], ACT.Copy).then_inc(y_act, 1)
                    for t in range(TT):
                        act.drain()
                        act.wait_ge(added, m * (4 * TT) + (TT * b + t + 2))
                        act.activation(squares, x_cols[:, t, b], ACT.Square, accum_out=ssq[:, t, b:b + 1])
                act.drain().then_inc(round_squared, 1)

            with act.Fori(0, GROUPS) as g:
                experts(g)
            act.wait_ge(passes_made, 1)
            passes = act.value_load(passes_i[0:1, 0:1], min_val=1, max_val=MAX_PASSES)
            with act.If(passes > 1):
                with act.Fori(1, passes) as again:
                    with act.Fori(0, GROUPS) as g:
                        experts(again * GROUPS + g)

        @block.vector
        def _(dve):
            dve.sem_inc(proj_dve, 2)
            dve.sem_inc(heads_stored, 1)
            dve.sem_inc(added, 1)
            dve.sem_inc(place_turned, 1)

            def inverse_root(out_):
                bits, guess = newton[:].bitcast(I32), out_.bitcast(I32)
                dve.tensor_single_scalar(bits, var[:].bitcast(I32), 1, op=ALU.logical_shift_right)
                dve.drain()
                dve.tensor_scalar(guess, bits, -1.0, float(0x5f3759df), ALU.mult, ALU.add)
                for _ in range(3):
                    dve.drain()
                    dve.tensor_tensor(newton[:], out_, out_, ALU.mult)
                    dve.drain()
                    dve.scalar_tensor_tensor(out=newton[:], in0=newton[:], scalar=-0.5, in1=var[:],
                                             op0=ALU.mult, op1=ALU.mult)
                    dve.drain()
                    dve.scalar_tensor_tensor(out=out_, in0=newton[:], scalar=1.5, in1=out_,
                                             op0=ALU.add, op1=ALU.mult)

            def norm(parts, out_):
                if parts > 1:
                    dve.tensor_reduce(var[:], ssq[:, :, 0:parts], AX, ALU.add)
                    dve.drain()
                    dve.tensor_scalar(var[:], var[:], 1.0 / D, EPS, ALU.mult, ALU.add)
                else:
                    dve.tensor_scalar(var[:], ssq[:, :, 0], 1.0 / D, EPS, ALU.mult, ALU.add)
                dve.drain()
                inverse_root(out_)
                dve.drain()

            dve.wait_ge(g_mix_in, 16)
            for n in range(4 * TT):
                t, m = n // 4, n % 4
                dve.wait_ge(x_turned, n + 1)
                dve.tensor_tensor(hT[:, 4 * m:4 * m + 4, t * P:(t + 1) * P],
                                  bank[n][:].rearrange("p (k s) -> p k s", k=4),
                                  g_mix_sb[:, 4 * m:4 * m + 4].unsqueeze(2).broadcast_to([P, 4, P]),
                                  ALU.mult).then_inc(xT_made, 1)
            dve.wait_ge(squared, 1)
            norm(1, rstd_in[:])
            dve.sem_inc(rstd_made, 1)
            dve.wait_ge(early_in, 16 * 3)
            lam_prod = stick[:, 0:2 * HQ].rearrange("p (a b) -> p a b", a=2)
            lam_v = lam_sb[:, :, :].rearrange("p (a b) d -> p a b d", b=2)
            dve.tensor_tensor(lam_prod, lam_v[:, :, 0], lam_v[:, :, 1], ALU.mult)
            dve.drain()
            dve.tensor_reduce(lam_two[:], lam_prod, AX, ALU.add).then_inc(lam_summed, 1)
            dve.wait_ge(lam_exped, 1)
            dve.tensor_scalar(neg_lam[:], lam_two[:, 0:1], -1.0, -LAMBDA_INIT, ALU.mult, ALU.add)
            dve.drain()
            dve.tensor_tensor(neg_lam[:], neg_lam[:], lam_two[:, 1:2], ALU.add)
            dve.tensor_scalar(gsub[:], gsub[:], 1.0 - LAMBDA_INIT, None, ALU.mult)
            dve.wait_ge(masks_made, 1)
            dve.tensor_copy(pos_f[:], pos_i[:])
            dve.drain()
            for t in range(TT):
                dve.tensor_scalar(angle[:, t], inv_freq[:], pos_f[:, t:t + 1], None, ALU.mult)
            dve.drain()
            dve.tensor_scalar(whole[:], angle[:], float(1 / (2 * np.pi)), None, ALU.mult)
            dve.drain()
            dve.tensor_scalar(whole[:], whole[:], ROUND, None, ALU.add)
            dve.drain()
            dve.tensor_scalar(whole[:], whole[:], -ROUND, None, ALU.add)
            for c in TWO_PI:
                dve.drain()
                dve.scalar_tensor_tensor(out=angle[:], in0=whole[:], scalar=-c, in1=angle[:],
                                         op0=ALU.mult, op1=ALU.add)
            dve.drain()
            dve.tensor_scalar(angle[:], angle[:], 3.1415925, -3.1415925, ALU.min, ALU.max).then_inc(angles_made, 1)
            dve.wait_ge(angles_made, 2)
            dve.tensor_tensor(cos[:], cos[:], cos[:], ALU.mult)
            dve.drain()
            dve.tensor_scalar(cos[:], cos[:], -2.0, 1.0, ALU.mult, ALU.add)
            dve.drain()
            dve.wait_ge(sines_made, 1)
            dve.sem_inc(sines_made, 1)

            def copy_block(n, j, dst):
                dve.wait_ge(slots_used, (n + 1) * 2 + RING)
                dve.tensor_scalar(dst, bank[2 * j + 1][:], rstd_in[:, 1:2], None, ALU.mult).then_inc(proj_dve, 1)

            with dve.Fori(0, TURN_GATE) as i:
                for j in range(PAIR):
                    copy_block(i * PAIR + j, j, qkv_cols[:, 1].rearrange("p (i j) n -> p i j n", j=PAIR)[:, i, j])

            with dve.Fori(0, GATE_BLOCKS // PAIR) as i:
                for j in range(PAIR):
                    head = i * PAIR + j
                    dve.wait_ge(qk_turned, head + 2)
                    dve.tensor_copy(qkT[:, 2:4].rearrange("p a b -> p (a b)"), bank[5][:]).then_inc(qkT_dve, 1)
                    dve.wait_ge(diff_scored, head + 1)
                    for m in range(2):
                        dve.scalar_tensor_tensor(out=prob[:, m], in0=bank[6 + m][:, 0:3 * P], scalar=HQ ** -0.5,
                                                 in1=mask_upto[:], op0=ALU.mult, op1=ALU.add)
                    dve.drain()
                    dve.tensor_reduce(top[:, 0], prob[:, :, 0:P], AX, ALU.max)
                    dve.tensor_reduce(top[:, 1], prob[:, :, P:3 * P], AX, ALU.max)
                    dve.drain()
                    dve.tensor_scalar(neg_top[:], top[:], -1.0, None, ALU.mult).then_inc(tops_made, 1)
                    dve.wait_ge(sb_scored, head + 1)
                    dve.scalar_tensor_tensor(out=z[:], in0=bank[4][:, 0:3 * P], scalar=P ** -0.5,
                                             in1=mask_before[:], op0=ALU.mult, op1=ALU.add).then_inc(z_made, 1)
                    dve.wait_ge(diff_exped, head + 1)
                    dve.reciprocal(weight[:], total[:])
                    dve.drain()
                    dve.tensor_scalar(weight[:, :, 1], weight[:, :, 1], neg_lam[:], None, ALU.mult)
                    for t in range(TT):
                        c = slice(0, P) if t == 0 else slice(P, 3 * P)
                        dve.tensor_scalar(diff[:, c], prob[:, 0, c], weight[:, t, 0:1], None, ALU.mult)
                    dve.drain()
                    for t in range(TT):
                        c = slice(0, P) if t == 0 else slice(P, 3 * P)
                        dve.scalar_tensor_tensor(out=diff[:, c], in0=prob[:, 1, c], scalar=weight[:, t, 1:2],
                                                 in1=diff[:, c], op0=ALU.mult, op1=ALU.add)
                    dve.drain().then_inc(diff_made, 1)
                    dve.wait_ge(soft_made, head + 1)
                    dve.scalar_tensor_tensor(out=soft[:], in0=z[:], scalar=0.0, in1=soft[:],
                                             op0=ALU.max, op1=ALU.add)
                    dve.drain()
                    for c in (slice(0, P), slice(P, 3 * P)):
                        dve.tensor_tensor_scan(stick[:, c][:, ::-1], soft[:, c][:, ::-1], soft[:, c][:, ::-1],
                                               0.0, ALU.add, ALU.max)
                    dve.drain()
                    dve.tensor_tensor(stick[:], z[:], stick[:], ALU.subtract).then_inc(stick_summed, 1)
                    dve.wait_ge(sb_turned, head + 1)
                    dve.tensor_copy(aT_sb[:], bank[6][:, 0:3 * P]).then_inc(aT_dve, 1)
                    dve.wait_ge(head_squared, head + 1)
                    dve.tensor_scalar(var[:], ssq[:, :, 0], 1.0 / HV, EPS, ALU.mult, ALU.add)
                    dve.tensor_copy(qkv[:, :, SQ].rearrange("p t h d -> p h t d")[:, head],
                                    bank[7][:, T:2 * T].rearrange("p (t d) -> p t d", t=TT))
                    dve.drain()
                    inverse_root(rstd[:])
                    dve.drain()
                    for t in range(TT):
                        dve.scalar_tensor_tensor(out=qkv[:, t, DQ][:, head], in0=bank[7][:, t * P:(t + 1) * P],
                                                 scalar=rstd[:, t:t + 1], in1=gsub[:], op0=ALU.mult, op1=ALU.mult)
                    dve.drain()
                    dve.sem_inc(heads_stored, 1)
                    copy_block(head + IN_BLOCKS, j,
                               gate_cols[:, 1].rearrange("p (i j) n -> p i j n", j=PAIR)[:, i, j])

            for m in range(1, KH, 2):
                dve.wait_ge(turned, m + 1)
                for k in range(2):
                    dve.tensor_copy(hT[:, 2 * m + k], bank[4 + m % 4][:, k * T:(k + 1) * T]).then_inc(turned_dve, 1)
            dve.wait_ge(gates_open, 1)
            for n in range(2 * OUT_BLOCKS):
                pair = 2 * (n % 3)
                dve.wait_ge(slots_used, RING * (TURN_BR + 1) + n + 1)
                for t in range(TT):
                    g = gate_cols[:, t, (n % 2) * OUT_BLOCKS + n // 2]
                    dve.tensor_tensor(g, g, bank[pair + t][:], ALU.mult)
                dve.drain()
                if n % 2 == 0:
                    dve.sem_inc(mixed, 1)
                else:
                    for t in range(TT):
                        g0, g1 = gate_cols[:, t, n // 2], gate_cols[:, t, OUT_BLOCKS + n // 2]
                        dve.tensor_tensor(g0, g0, g1, ALU.add)
                    dve.drain().then_inc(mixed, 1)
            for n in range(OUT_BLOCKS):
                pair = 2 * (n % 2)
                dve.wait_ge(slots_used, RING * (TURN_OUT + 1) + 2 * n + 2)
                for t in range(TT):
                    dve.tensor_tensor(x_cols[:, t, n], x_cols[:, t, n], bank[pair + t][:], ALU.add).then_inc(x_added, 1)
                if n == 0:
                    dve.wait_ge(route_in, 16 * 5)
                if n == OUT_BLOCKS - 1:
                    break
                dve.wait_ge(turned, KH + 2 * n + 2)
                for k in range(2):
                    dve.tensor_scalar(hT[:, 4 * n + 2 + k], bank[5][:, k * T:(k + 1) * T],
                                      g_moe_sb[:, 4 * n + 2 + k:4 * n + 3 + k], None, ALU.mult).then_inc(turned_dve, 1)
            dve.wait_ge(squared, 2)
            norm(OUT_BLOCKS, rstd[:])
            dve.sem_inc(rstd_made, 1)

            def bc(v, n):
                return v.broadcast_to([P, TT, n])

            def first_max(out_, values, top_, n):
                dve.tensor_tensor(out_, values, bc(top_, n), ALU.is_equal)
                dve.drain()
                fall = falling[:].unsqueeze(1).broadcast_to([P, TT, n])
                dve.tensor_tensor(tie[:, :, 0:n], out_, fall, ALU.mult)
                dve.drain()
                dve.tensor_reduce(tie_top, tie[:, :, 0:n], AX, ALU.max)
                dve.drain()
                dve.tensor_tensor(out_, tie[:, :, 0:n], bc(tie_top, n), ALU.is_equal)
                dve.drain()

            dve.wait_ge(logits_made, 1)
            for t in range(TT):
                dve.scalar_tensor_tensor(out=logits[:, t], in0=bank[6 + t][:, 0:NG + NE], scalar=rstd[:, t:t + 1],
                                         in1=b_route[:], op0=ALU.mult, op1=ALU.add)
            dve.drain()
            dve.tensor_reduce(best[:, :, 0:1], logits[:, :, 0:NG], AX, ALU.max)
            dve.drain()
            first_max(is_group, logits[:, :, 0:NG], best[:, :, 0:1], NG)
            dve.tensor_tensor(shifted[:, :, 0:NG], logits[:, :, 0:NG], bc(best[:, :, 0:1], NG),
                              ALU.subtract).then_inc(route_shifted, 1)
            dve.tensor_scalar(is_group, is_group, BIG, -BIG, ALU.mult, ALU.add)
            dve.drain()
            for t in range(TT):
                dve.tensor_tensor(masked[:, t].rearrange("p (g e) -> p g e", g=NG),
                                  logits[:, t, NG:].rearrange("p (g e) -> p g e", g=NG),
                                  is_group[:, t].unsqueeze(2).broadcast_to([P, NG, PER]), ALU.add)
            dve.drain()
            for t in range(TT):
                dve.max(best8[:, t], masked[:, t])
            dve.drain()
            for t in range(TT):
                dve.max_index(place8[:, t], best8[:, t], masked[:, t])
            dve.drain()
            dve.tensor_copy(best_at, place8[:, :, 0:2])
            dve.drain()
            for c in range(2):
                dve.tensor_tensor(is_top[c], expert_id[:].unsqueeze(1).broadcast_to([P, TT, NE]),
                                  bc(best_at[:, :, c:c + 1], NE), ALU.is_equal)
            dve.drain()
            dve.tensor_tensor(chosen_b[:], is_top[0], is_top[1], ALU.add).then_inc(chosen_made, 1)
            dve.tensor_tensor(shifted[:, :, NG:NG + 1], best8[:, :, 1:2], best8[:, :, 0:1], ALU.subtract).then_inc(route_shifted, 1)
            dve.tensor_tensor(chosen, is_top[0], is_top[1], ALU.add)
            dve.drain()
            dve.wait_ge(route_exped, 2)
            dve.scalar_tensor_tensor(out=pair_w[:, :, 1:2], in0=shifted[:, :, NG:NG + 1], scalar=1.0,
                                     in1=pair_w[:, :, 0:1], op0=ALU.add, op1=ALU.mult)
            dve.drain()
            dve.reciprocal(pair_w[:, :, 2:3], pair_w[:, :, 1:2])
            dve.drain().then_inc(first_weighed, 1)
            dve.wait_ge(ranks_made, 1)
            dve.scalar_tensor_tensor(out=rank, in0=bank[1][:, 0:TT * NE].rearrange("p (t n) -> p t n", t=TT),
                                     scalar=float(2 * T), in1=chosen, op0=ALU.add, op1=ALU.mult)
            dve.tensor_reduce(count[:, 0:1], bank[1][:, TT * NE:(TT + 1) * NE], AX, ALU.max)
            dve.drain().then_inc(count_made, 1)
            dve.tensor_scalar(rank, rank, -float(2 * T), None, ALU.add)
            dve.drain()

            def experts(m, g):
                dve.drain()
                dve.wait_ge(place_turned, m + 1)
                def by_expert(v, t):
                    return (v[:, t].rearrange("p (g e) -> p g e", e=SIDE)[:, g]
                            .unsqueeze(2).broadcast_to([P, SIDE, SLOTS]))

                def by_slot(n, t):
                    return pick[:, n, t].rearrange("p (e s) -> p e s", e=SIDE)

                for t in range(TT):
                    dve.tensor_tensor(by_slot(0, t), slot_id[:].unsqueeze(1).broadcast_to([P, SIDE, SLOTS]),
                                      by_expert(rank, t), ALU.is_equal)
                dve.drain().then_inc(picks_made, 1)
                dve.wait_ge(combine_made, 1)
                for t in range(TT):
                    dve.tensor_tensor(by_slot(1, t), by_slot(0, t), by_expert(combine, t), ALU.mult)
                dve.drain().then_inc(places_made, 1)
                for q in range(KH):
                    dve.wait_ge(gathered, m * KH + q + 1)
                    dve.tensor_tensor(xgT[:, 2 * q:2 * q + 2],
                                      bank[2 + q % 2][:, 0:2 * P].rearrange("p (k s) -> p k s", k=2),
                                      g_moe_sb[:, 2 * q:2 * q + 2].unsqueeze(2).broadcast_to([P, 2, P]),
                                      ALU.mult).then_inc(xg_made, 1)
                dve.wait_ge(silu_made, m + 1)
                dve.tensor_tensor(act_sb[:, 1], act_sb[:, 0], bank[1][:], ALU.mult).then_inc(act_made, 1)
                for b in range(OUT_BLOCKS):
                    if b % 2 == 0:
                        dve.wait_ge(slots_used, m * LOADS + (RING + USED_MOE + KD + 2 * (b + 1)))
                        dve.tensor_copy(y_sb[:, b * BLK:(b + 1) * BLK], bank[4 + b][:]).then_inc(y_dve, 1)
                    for t in range(TT):
                        dve.wait_ge(combined, m * (4 * TT) + (TT * b + t + 1))
                        dve.tensor_tensor(x_cols[:, t, b], x_cols[:, t, b], bank[(2 + TT * b + t) % 4][:],
                                          ALU.add).then_inc(added, 1)

            with dve.Fori(0, GROUPS) as g:
                experts(g, g)
            dve.wait_ge(passes_made, 1)
            passes = dve.value_load(passes_i[0:1, 0:1], min_val=1, max_val=MAX_PASSES)
            with dve.If(passes > 1):
                dve.drain()
                dve.tensor_scalar(rank, rank, -float(SLOTS), None, ALU.add)
                with dve.Fori(1, passes) as again:
                    with dve.Fori(0, GROUPS) as g:
                        experts(again * GROUPS + g, g)
                    dve.drain()
                    dve.wait_ge(round_squared, again * GROUPS + GROUPS)
                    dve.tensor_scalar(rank, rank, -float(SLOTS), None, ALU.add)
            dve.drain()
            dve.wait_ge(round_squared, GROUPS)
            norm(OUT_BLOCKS, rstd[:])
            dve.wait_ge(g_final_in, 16)
            for t, c in [(t, slice(c, c + BLK)) for t in range(TT) for c in range(0, D, BLK)]:
                dve.scalar_tensor_tensor(out=normed[:, t, c], in0=x_tok[:, t, c], scalar=rstd[:, t:t + 1],
                                         in1=g_final_sb[:, c], op0=ALU.mult, op1=ALU.mult).then_inc(out_made, 1)


_INS = ["x", "positions", "g_mix", "w_in", "w_gate", "lambda_params", "g_subln", "w_br_diff",
        "w_br_sb", "w_out", "g_moe", "w_group", "b_group", "w_router", "b_router", "w_up_gate",
        "w_up", "w_down", "g_final"]


def kernel(**inputs):
    import numpy as _np
    import concourse.bacc as _bacc
    from concourse import mybir as _mybir
    from concourse.bass_utils import run_bass_kernel_spmd as _run

    nc = _bacc.Bacc("TRN2", target_bir_lowering=False, num_devices=1)
    arrays, args = {}, []
    for name in _INS:
        a = _np.ascontiguousarray(inputs[name])
        arrays[f"in_{name}"] = a
        args.append(nc.dram_tensor(f"in_{name}", a.shape, _mybir.dt.from_np(a.dtype), kind="ExternalInput").ap())
    out = nc.dram_tensor("block_out", inputs["x"].shape, _mybir.dt.float32, kind="ExternalOutput").ap()
    decoder_block(nc, *args, out)
    r = _run(nc, [arrays], core_ids=[0])
    return r.results[0]["block_out"]
```

```python
from contextlib import ExitStack

import numpy as np

import concourse.bass as bass
from concourse import mybir
from concourse.alu_op_type import AluOpType as ALU

F32 = mybir.dt.float32
I32 = mybir.dt.int32
BF16 = mybir.dt.bfloat16
ACT = mybir.ActivationFunctionType
AX = mybir.AxisListType.X

P = 128
BLK = 512
ROPE_THETA = 500000.0
EPS = 1e-6
LAMBDA_INIT = 0.8 - 0.6 * float(np.exp(-0.3 * 0))
BIG = 1e30
RING = 4
MORE = 4
SLOTS = 32
SIDE = 4
TWO_PI = (6.28125, 0.0019350051879882812, 3.0199159819e-07)
ROUND = float(3 << 22)
TYPES = 6
DQ, DK, DV, SQ, SK, SV = range(TYPES)


def decoder_block(nc, x, positions, g_mix, w_in, w_gate, lambda_params, g_subln, w_br_diff,
                  w_br_sb, w_out, g_moe, w_group, b_group, w_router, b_router, w_up_gate, w_up,
                  w_down, g_final, out):
    _, T, D = x.shape
    TT = T // P
    KD = D // P
    HV = g_subln.shape[1]
    HQ = lambda_params.shape[2]
    HEADS = w_br_diff.shape[1] // HV
    HALF = HQ // 4 // 2
    NG = w_group.shape[2]
    NE = w_router.shape[2]
    PER = NE // NG
    FF = w_up.shape[3]
    IN_BLOCKS = w_in.shape[2] // BLK
    GATE_BLOCKS = w_gate.shape[2] // BLK
    OUT_BLOCKS = D // BLK
    assert TT == 2 and HV == P and 2 * HQ == P and w_in.shape[2] == TYPES * HEADS * P
    assert GATE_BLOCKS == HEADS and FF == BLK and OUT_BLOCKS == 4 and KD == 16
    KH = KD // 2
    PAIR = 2
    GROUPS = NE // SIDE
    MAX_PASSES = T // SLOTS
    TURN_GATE = IN_BLOCKS // PAIR
    TURN_BR = TURN_GATE + GATE_BLOCKS // PAIR
    TURN_OUT = TURN_BR + 2 * OUT_BLOCKS // RING
    TURN_MOE = TURN_OUT + 2 * OUT_BLOCKS // RING
    USED_MOE = RING * TURN_MOE
    LOADS = KD + 2 * (FF // P)
    MOE_RING = RING + MORE
    MOE_TURNS = LOADS // MOE_RING
    assert LOADS % MOE_RING == 0

    ctx = ExitStack()
    with ctx:
        def sb(name, shape, dt=F32):
            return ctx.enter_context(nc.sbuf_tensor(name, shape, dt))

        def sem(name):
            return ctx.enter_context(nc.semaphore(name))

        ring = sb("ring", [P, RING, KH * BLK])
        x_tok = sb("x_tok", [P, TT, D])
        hT = sb("hT", [P, KD, T])
        qkv = sb("qkv", [P, TT, TYPES, HEADS, P])
        gates = sb("gates", [P, TT, 2 * D])
        small_mem = sb("small_mem", [P, 5120])

        def part(flat, at, *shape):
            n = int(np.prod(shape))
            v = flat[:, at:at + n]
            if len(shape) == 2:
                return v.rearrange("p (a b) -> p a b", a=shape[0])
            if len(shape) == 3:
                return v.rearrange("p (a b c) -> p a b c", a=shape[0], b=shape[1])
            return v

        diffT = qkv[:, 0, DQ:DK + 1, :, :].rearrange("p t h s -> p h t s")
        sbT = qkv[:, 0, SQ:SK + 1, :, :].rearrange("p t h s -> p h t s")
        SLOT = KH * BLK
        qkv_flat = qkv[:, :, :, :, :].rearrange("p a b c d -> p (a b c d)")
        normed = part(qkv_flat, 0, TT, D)
        x2T = part(qkv_flat, 0, KD, T)
        junk = part(qkv_flat, SLOT, D)
        gates_flat = gates[:, :, :].rearrange("p a b -> p (a b)")
        rope_tmp = part(gates_flat, 0, 4, 2 * 2 * HEADS, HALF)
        slots = [ring[:, s] for s in range(RING)] + [part(qkv_flat, (1 + s) * SLOT, SLOT) for s in range(2)] \
            + [part(gates_flat, s * SLOT, SLOT) for s in range(2)]
        mixT = hT
        hT_flat = hT[:, :, :].rearrange("p a b -> p (a b)")
        xgT = part(hT_flat, 0, KD, P)
        y_sb = part(hT_flat, KD * P, D)
        stage = part(small_mem, 0, TT, 4, P)
        qkT = part(small_mem, 1024, 4, T)
        prob = part(small_mem, 2048, 2, 3 * P)
        diff, z, soft, stick, aT_diff, aT_sb = (part(small_mem, 2816 + n * 3 * P, 3 * P) for n in range(6))
        act_sb = part(small_mem, 0, 2, BLK)
        squares = part(small_mem, 0, BLK)
        actT = part(small_mem, 1024, FF // P, P)
        pick = part(small_mem, 1536, 2, TT, P)
        placeT = part(small_mem, 2048, T)
        g_final_sb = part(small_mem, 2304, D)
        routing = part(small_mem, 4352, 768)
        at = [0]

        def small(*shape):
            v = part(routing, at[0], *shape)
            at[0] += int(np.prod(shape))
            return v

        logits = small(TT, NG + NE)
        best = small(TT, 1)
        best8 = small(TT, 8)
        best_at = small(TT, 2)
        shifted = small(TT, NG + 1)
        is_other = small(TT, NG)
        masked = small(TT, NE)
        is_top = [small(TT, NE), small(TT, NE)]
        tie = small(TT, NG)
        tie_top = small(TT, 1)
        chosen = small(TT, NE)
        combine = small(TT, NE)
        rank = small(TT, NE)
        pair_w = small(TT, 4)
        over = small(MAX_PASSES - 1)
        count = small(2)

        ident = sb("ident", [P, P])
        before = sb("before", [P, P])
        ones = sb("ones", [P, P])
        before_b = sb("before_b", [P, P], BF16)
        ones_b = sb("ones_b", [P, P], BF16)
        chosen_b = sb("chosen_b", [P, TT, NE], BF16)
        mask_upto = sb("mask_upto", [P, 3 * P])
        mask_before = sb("mask_before", [P, 3 * P])
        gsub = sb("gsub", [P, HV])
        slot_id = sb("slot_id", [P, SLOTS])
        falling = sb("falling", [P, NG])
        expert_id = sb("expert_id", [P, NE])
        starts = sb("starts", [P, MAX_PASSES - 1])
        inv_freq = sb("inv_freq", [P, HALF])
        g_mix_sb = sb("g_mix_sb", [P, KD])
        g_moe_sb = sb("g_moe_sb", [P, KD])
        w_route = sb("w_route", [P, KD, NG + NE])
        b_route = sb("b_route", [P, NG + NE])
        lam_sb = sb("lam_sb", [P, 4, HQ])
        pos_i = sb("pos_i", [P, TT], I32)
        passes_i = sb("passes_i", [P, 1], I32)
        place8 = sb("place8", [P, TT, 8], mybir.dt.uint32)
        sv_stage = sb("sv_stage", [P, TT, P])
        pos_f = sb("pos_f", [P, TT])
        angle = sb("angle", [P, TT, HALF])
        whole = sb("whole", [P, TT, HALF])
        sin = sb("sin", [P, TT, HALF])
        cos = sb("cos", [P, TT, HALF])
        lam_two = sb("lam_two", [P, 2])
        neg_lam = sb("neg_lam", [P, 1])
        top = sb("top", [P, TT, 2])
        neg_top = sb("neg_top", [P, TT, 2])
        total = sb("total", [P, TT, 2])
        weight = sb("weight", [P, TT, 2])
        ssq = sb("ssq", [P, TT, OUT_BLOCKS])
        sums = sb("sums", [P, TT])
        var = sb("var", [P, TT])
        minus_half = sb("minus_half", [P, TT])
        rstd_in = sb("rstd_in", [P, TT])
        rstd = sb("rstd", [P, TT])
        newton = sb("newton", [P, TT])

        bank = [ctx.enter_context(nc.psum_tensor(f"bank{i}", [P, BLK], F32)) for i in range(8)]

        x_in = [sem(f"x_in{t}") for t in range(TT)]
        g_mix_in = sem("g_mix_in")
        early_in = sem("early_in")
        route_in = sem("route_in")
        g_final_in = sem("g_final_in")
        out_written = sem("out_written")
        slot_full = [[sem(f"slot_full{i}_{q}") for q in range(2)] for i in range(RING + MORE)]
        slots_used = sem("slots_used")
        masks_made = sem("masks_made")
        sines_made = sem("sines_made")
        angles_made = sem("angles_made")
        lam_summed = sem("lam_summed")
        lam_exped = sem("lam_exped")
        squared = sem("squared")
        rstd_made = sem("rstd_made")
        round_squared = sem("round_squared")
        normed_made = sem("normed_made")
        x_turned = sem("x_turned")
        xT_made = sem("xT_made")
        turned = sem("turned")
        turned_act = sem("turned_act")
        turned_dve = sem("turned_dve")
        proj_act = sem("proj_act")
        proj_dve = sem("proj_dve")
        staged = sem("staged")
        qk_turned = sem("qk_turned")
        qkT_act = sem("qkT_act")
        qkT_dve = sem("qkT_dve")
        diff_scored = sem("diff_scored")
        sb_scored = sem("sb_scored")
        tops_made = sem("tops_made")
        z_made = sem("z_made")
        diff_exped = sem("diff_exped")
        soft_made = sem("soft_made")
        stick_summed = sem("stick_summed")
        stick_exped = sem("stick_exped")
        diff_made = sem("diff_made")
        diff_turned = sem("diff_turned")
        sb_turned = sem("sb_turned")
        aT_act = sem("aT_act")
        aT_dve = sem("aT_dve")
        diff_out = sem("diff_out")
        sb_out = sem("sb_out")
        v_staged = sem("v_staged")
        head_squared = sem("head_squared")
        head_normed = sem("head_normed")
        head_turned = sem("head_turned")
        diffT_act = sem("diffT_act")
        sbT_dve = sem("sbT_dve")
        gates_open = sem("gates_open")
        mixed = sem("mixed")
        mix_turned = sem("mix_turned")
        mixT_made = sem("mixT_made")
        x_added = sem("x_added")
        logits_made = sem("logits_made")
        route_shifted = sem("route_shifted")
        route_exped = sem("route_exped")
        first_weighed = sem("first_weighed")
        combine_made = sem("combine_made")
        chosen_made = sem("chosen_made")
        ranks_made = sem("ranks_made")
        passes_made = sem("passes_made")
        count_made = sem("count_made")
        picks_made = sem("picks_made")
        places_made = sem("places_made")
        gathered = sem("gathered")
        xg_made = sem("xg_made")
        place_turned = sem("place_turned")
        placeT_made = sem("placeT_made")
        silu_made = sem("silu_made")
        act_made = sem("act_made")
        act_turned = sem("act_turned")
        actT_made = sem("actT_made")
        y_act = sem("y_act")
        y_dve = sem("y_dve")
        combined = sem("combined")
        added = sem("added")
        out_made = sem("out_made")

        x_d = x[0].rearrange("(t p) d -> t p d", p=P)
        out_d = out[0].rearrange("(t p) d -> t p d", p=P)
        w_in_d = w_in[0].rearrange("(h q k p) (b n) -> h q b p k n", h=2, q=2, p=P, n=BLK)
        w_gate_d = w_gate[0].rearrange("(h q k p) (b n) -> h q b p k n", h=2, q=2, p=P, n=BLK)
        w_out_d = w_out[0].rearrange("(h q k p) (b n) -> h q b p k n", h=2, q=2, p=P, n=BLK)
        w_br_d = [w[0].rearrange("(q k p) (b n) -> q b p k n", q=2, p=P, n=BLK)
                  for w in (w_br_diff, w_br_sb)]
        up_d = [w[0].rearrange("(g e) (k p) n -> k g p e n", e=SIDE, p=P) for w in (w_up_gate, w_up)]
        down_d = w_down[0].rearrange("(g e) (f u p) (b n) -> b f u g p e n", e=SIDE, u=2, p=P, n=BLK)

        def slot(s):
            return slots[s].rearrange("p (k n) -> p k n", n=BLK)

        qkv_cols = qkv[:, :, :, :, :].rearrange("p t a (c h) d -> p t (a c) (h d)", c=2)
        gate_cols = gates[:, :, :].rearrange("p t (b n) -> p t b n", n=BLK)
        x_cols = x_tok[:, :, :].rearrange("p t (b n) -> p t b n", n=BLK)

        def vec(a):
            return a.rearrange("a (k p) -> p (a k)", p=P)

        block = ctx.enter_context(nc.Block())

        @block.sync
        def _(sp):
            sp.sem_inc(slots_used, RING)
            for t in range(TT):
                sp.dma_start(x_tok[:, t], x_d[t]).then_inc(x_in[t], 16)

            def fill(s, quarters):
                for q, src in reversed(list(enumerate(quarters))):
                    dst = slots[s][:, q * 4 * BLK:(q + 1) * 4 * BLK]
                    dst = dst.rearrange("p (k n) -> p k n", k=src.shape[1])
                    sp.dma_start(dst, src).then_inc(slot_full[s][q], 16)

            def load(s, turn, quarters):
                sp.wait_ge(slots_used, RING * turn + s + 1)
                fill(s, quarters)

            def expert_quarters(n, g, ahead=0):
                if n < KD:
                    return [w[n, ahead:][g] for w in up_d]
                n -= KD
                return [down_d[n // 2, n % 2, u, ahead:][g] for u in range(2)]

            def load_experts(g, m, loads, ahead=0):
                for n in loads:
                    sp.wait_ge(slots_used, m * LOADS + (USED_MOE + RING + n - MOE_RING + 1 + ahead * LOADS))
                    fill((n + RING) % MOE_RING, expert_quarters(n, g, ahead))

            with sp.Fori(0, TURN_GATE) as i:
                for s in range(RING):
                    load(s, i, [w_in_d[s % 2, q].rearrange("(i j) p k n -> i j p k n", j=PAIR)[i, s // 2]
                                for q in range(2)])
            with sp.Fori(0, GATE_BLOCKS // PAIR) as i:
                for s in range(RING):
                    load(s, i + TURN_GATE, [w_gate_d[s % 2, q].rearrange("(i j) p k n -> i j p k n", j=PAIR)[i, s // 2]
                                            for q in range(2)])
            for n in range(2 * OUT_BLOCKS):
                load(n % RING, TURN_BR + n // RING, [w_br_d[1 - n % 2][q, n // 2] for q in range(2)])
            sp.wait_ge(sb_out, 1 + HEADS)
            fill(RING + 1, expert_quarters(1, 0))
            for n in range(2 * OUT_BLOCKS):
                if n == RING:
                    sp.wait_ge(mix_turned, 2 * OUT_BLOCKS)
                load(n % RING, TURN_OUT + n // RING, [w_out_d[n % 2, q, n // 2] for q in range(2)])
                if n >= RING and n != RING + 1:
                    fill(n, expert_quarters(n - RING, 0))
            with sp.Fori(0, GROUPS - 1) as g:
                load_experts(g, g, range(MORE, LOADS))
                load_experts(g, g, range(MORE), ahead=1)
            load_experts(GROUPS - 1, GROUPS - 1, range(MORE, LOADS))
            sp.wait_ge(passes_made, 1)
            passes = sp.value_load(passes_i[0:1, 0:1], min_val=1, max_val=MAX_PASSES)
            with sp.If(passes > 1):
                with sp.Fori(1, passes) as again:
                    with sp.Fori(0, GROUPS) as g:
                        load_experts(g, again * GROUPS + g, range(LOADS))
            for n in range(OUT_BLOCKS * TT):
                t, c = n // OUT_BLOCKS, slice(n % OUT_BLOCKS * BLK, (n % OUT_BLOCKS + 1) * BLK)
                sp.wait_ge(out_made, n + 1)
                sp.dma_start(out_d[t][:, c], normed[:, t, c]).then_inc(out_written, 16)
            sp.wait_ge(out_written, 16 * OUT_BLOCKS * TT)

        @block.gpsimd
        def _(pool):
            pool.sem_inc(qk_turned, 1)
            pool.sem_inc(sb_out, 1)
            pool.memset(ident[:], 0.0)
            pool.memset(ones[:], 1.0)
            pool.memset(mask_upto[:], 0.0)
            pool.memset(mask_before[:], 0.0)
            for i in range(HALF):
                f = np.float32(ROPE_THETA) ** np.float32(-2.0 * i / (2 * HALF))
                pool.memset(inv_freq[:, i:i + 1], float(f))
            pool.iota(slot_id[:], [[1, SLOTS]], base=0, channel_multiplier=0,
                      allow_small_or_imprecise_dtypes=True)
            pool.iota(expert_id[:], [[1, NE]], base=0, channel_multiplier=0,
                      allow_small_or_imprecise_dtypes=True)
            pool.iota(falling[:], [[-1, NG]], base=NG, channel_multiplier=0,
                      allow_small_or_imprecise_dtypes=True)
            pool.iota(starts[:], [[SLOTS, MAX_PASSES - 1]], base=SLOTS, channel_multiplier=0,
                      allow_small_or_imprecise_dtypes=True)
            pool.drain()
            pool.affine_select(out=ident[:], in_=ident[:], compare_op=ALU.not_equal, fill=1.0,
                               base=0, pattern=[[-1, P]], channel_multiplier=1)
            pool.affine_select(out=before[:], in_=ones[:], compare_op=ALU.is_ge, fill=0.0,
                               base=-1, pattern=[[1, P]], channel_multiplier=-1)
            for m, off in ((mask_upto, 0), (mask_before, -1)):
                for c in (0, 2 * P):
                    pool.affine_select(out=m[:, c:c + P], in_=m[:, c:c + P], compare_op=ALU.is_ge,
                                       fill=-BIG, base=off, pattern=[[-1, P]], channel_multiplier=1)
            pool.tensor_copy(ones_b[:], ones[:])
            pool.drain()
            pool.tensor_copy(before_b[:], before[:])
            pool.drain().then_inc(masks_made, 1)
            with nc.allow_non_contiguous_dma("small vectors"):
                pool.dma_start(g_moe_sb[:], vec(g_moe)).then_inc(route_in, 16)
                pool.dma_start(w_route[:, :, 0:NG],
                               w_group[0].rearrange("(k p) n -> p k n", p=P)).then_inc(route_in, 16)
                pool.dma_start(w_route[:, :, NG:],
                               w_router[0].rearrange("(k p) n -> p k n", p=P)).then_inc(route_in, 16)
                pool.dma_start(b_route[:, 0:NG], b_group[0].partition_broadcast(P)).then_inc(route_in, 16)
                pool.dma_start(b_route[:, NG:], b_router[0].partition_broadcast(P)).then_inc(route_in, 16)

            rope_blocks = 2 * HEADS * P // BLK
            pool.wait_ge(sines_made, 2)
            pool.wait_ge(proj_act, 2 + rope_blocks)
            pool.wait_ge(proj_dve, 2 + rope_blocks)
            for t in range(TT):
                qk = qkv[:, t, DQ:DK + 1, :, :].rearrange("p a h (c d) -> p (a h c) d", c=2)
                first, second = qk[:, :, 0:HALF], qk[:, :, HALF:2 * HALF]
                c = cos[:, t].unsqueeze(1).broadcast_to([P, 4 * HEADS, HALF])
                s = sin[:, t].unsqueeze(1).broadcast_to([P, 4 * HEADS, HALF])
                if t:
                    pool.drain()
                pool.tensor_tensor(rope_tmp[:, 0], first, c, ALU.mult)
                pool.tensor_tensor(rope_tmp[:, 1], second, s, ALU.mult)
                pool.tensor_tensor(rope_tmp[:, 2], second, c, ALU.mult)
                pool.tensor_tensor(rope_tmp[:, 3], first, s, ALU.mult)
                pool.drain()
                pool.tensor_tensor(first, rope_tmp[:, 0], rope_tmp[:, 1], ALU.subtract)
                pool.tensor_tensor(second, rope_tmp[:, 2], rope_tmp[:, 3], ALU.add)
            pool.drain()
            pool.wait_ge(proj_act, 2 + SV * HEADS * P // BLK)
            pool.wait_ge(proj_dve, 2 + SV * HEADS * P // BLK)

            def stage_head(head):
                pool.wait_ge(qk_turned, head + 1)
                for n, a in enumerate((DQ, DK, SQ, SK)):
                    pool.tensor_copy(stage[:, :, n], qkv[:, :, a].rearrange("p t h d -> p h t d")[:, head])
                pool.drain().then_inc(staged, 1)
                pool.wait_ge(proj_act, 2 + IN_BLOCKS)
                pool.wait_ge(proj_dve, 2 + IN_BLOCKS)
                pool.wait_ge(sb_out, head + 1)
                pool.tensor_copy(sv_stage[:],
                                 qkv[:, :, SV].rearrange("p t h d -> p h t d")[:, head]).then_inc(v_staged, 1)

            with pool.Fori(0, HEADS) as head:
                stage_head(head)

            pool.wait_ge(x_added, TT * OUT_BLOCKS)
            pool.dma_start(g_final_sb, g_final.partition_broadcast(P)).then_inc(g_final_in, 16)

            pool.wait_ge(first_weighed, 1)
            pool.tensor_tensor(pair_w[:, :, 3:4], pair_w[:, :, 2:3], shifted[:, :, NG:NG + 1], ALU.mult)
            pool.drain()
            for c in range(2):
                pool.tensor_tensor(is_top[c], is_top[c], pair_w[:, :, 2 + c:3 + c].broadcast_to([P, TT, NE]),
                                   ALU.mult)
            pool.drain()
            pool.tensor_tensor(combine, is_top[0], is_top[1], ALU.add).then_inc(combine_made, 1)

            pool.wait_ge(count_made, 1)
            pool.tensor_scalar(over, starts[:], count[:, 0:1], None, ALU.is_lt)
            pool.drain()
            pool.tensor_scalar(count[:, 1:2], over[:, 0:1], 1.0, None, ALU.add)
            for n in range(1, MAX_PASSES - 1):
                pool.drain()
                pool.tensor_tensor(count[:, 1:2], count[:, 1:2], over[:, n:n + 1], ALU.add)
            pool.drain()
            pool.tensor_copy(passes_i[:], count[:, 1:2])
            pool.drain().then_inc(passes_made, 1)

        @block.tensor
        def _(pe):
            def turn_x2(n):
                pe.wait_ge(x_added, TT * (n + 1))
                for c in range(2):
                    if n:
                        pe.wait_ge((turned_act, turned_dve)[c], 2 * n)
                    for k in range(2):
                        for t in range(TT):
                            at = (2 * c + k) * P
                            mm = pe.transpose(bank[4 + c][:, k * T + t * P:k * T + (t + 1) * P],
                                              x_cols[:, t, n, at:at + P], ident[:])
                    mm.then_inc(turned, 1)

            def wait_dense(s, turn):
                for q in range(2):
                    pe.wait_ge(slot_full[s][q], 16 * (turn + 1))

            def route_block(n):
                last = n == OUT_BLOCKS - 1
                pe.wait_ge(turned_act, 2 * (n + 1))
                if not last:
                    pe.wait_ge(turned_dve, 2 * (n + 1))
                for k in range(4 * n, 4 * n + 4):
                    if last and k % 4 == 2:
                        pe.wait_ge(turned_act, 2 * (n + 2))
                    for t in range(TT):
                        mm = pe.matmul(bank[6 + t][:, 0:NG + NE], x2T[:, k, t * P:(t + 1) * P],
                                       w_route[:, k], start=(k == 0), stop=(k == KD - 1))
                return mm

            def project(n, j, turn, quarters):
                for step in range(4):
                    half, q = step // 2, 1 - step % 2
                    s = 2 * j + half
                    if step == 0:
                        pe.wait_ge(proj_act, n + 1)
                        pe.wait_ge(proj_dve, n + 1)
                    pe.wait_ge(slot_full[s][q], 16 * (turn + 1))
                    for k in range(4 * q, 4 * q + 4):
                        for t in range(TT):
                            mm = pe.matmul(bank[2 * j + t][:], hT[:, KH * half + k, t * P:(t + 1) * P],
                                           slot(s)[:, k], start=(step == 0 and k == 4 * q),
                                           stop=(step == 3 and k == 4 * q + 3))
                    if step % 2:
                        mm.then_inc(slots_used, 1)
                    quarters(step)

            pe.wait_ge(masks_made, 1)
            for t in range(TT):
                pe.wait_ge(x_in[t], 16)
                for m in range(4):
                    for k in range(4):
                        mm = pe.transpose(bank[4 * t + m][:, k * P:(k + 1) * P],
                                          x_tok[:, t, (4 * m + k) * P:(4 * m + k + 1) * P], ident[:])
                    mm.then_inc(x_turned, 1)
            pe.wait_ge(xT_made, 4 * TT)
            with pe.Fori(0, TURN_GATE) as i:
                for j in range(PAIR):
                    project(i * PAIR + j, j, i, lambda q: None)

            def attend(head, step):
                if step == 0:
                    pe.wait_ge(qkT_act, head + 1)
                    pe.wait_ge(qkT_dve, head + 1)
                    pe.wait_ge(diffT_act, head + 1)
                    pe.wait_ge(sbT_dve, head + 1)
                    for t in range(TT):
                        for m in range(2):
                            r, c = slice(m * HQ, (m + 1) * HQ), slice(t * P, (2 * t + 1) * P)
                            mm = pe.matmul(bank[6 + m][:, c], qkT[r, 0, t * P:(t + 1) * P],
                                           qkT[r, 1, 0:(t + 1) * P], start=True, stop=True)
                    mm.then_inc(diff_scored, 1)
                    pe.matmul(bank[4][:, 0:P], qkT[:, 2, 0:P], qkT[:, 3, 0:P], start=True, stop=True)
                    pe.matmul(bank[4][:, P:3 * P], qkT[:, 2, P:T], qkT[:, 3, :],
                              start=True, stop=True).then_inc(sb_scored, 1)
                if step == 1:
                    pe.wait_ge(diff_made, head + 1)
                    for c in range(3):
                        mm = pe.transpose(bank[5][:, c * P:(c + 1) * P], diff[:, c * P:(c + 1) * P], ident[:])
                    mm.then_inc(diff_turned, 1)
                if step == 2:
                    pe.wait_ge(aT_act, head + 1)
                    v = [qkv[:, t, DV][:, head] for t in range(TT)]
                    o = bank[7][:, 0:T]
                    pe.matmul(o[:, 0:P], aT_diff[:, 0:P], v[0], start=True, stop=True)
                    pe.matmul(o[:, P:T], aT_diff[:, P:2 * P], v[0], start=True, stop=False)
                    pe.matmul(o[:, P:T], aT_diff[:, 2 * P:3 * P], v[1],
                              start=False, stop=True).then_inc(diff_out, 1)
                    pe.wait_ge(stick_exped, head + 1)
                    for c in range(3):
                        mm = pe.transpose(bank[6][:, c * P:(c + 1) * P], stick[:, c * P:(c + 1) * P], ident[:])
                    mm.then_inc(sb_turned, 1)
                if step == 3:
                    pe.wait_ge(aT_dve, head + 1)
                    pe.wait_ge(v_staged, head + 1)
                    pe.wait_ge(head_normed, head + 1)
                    o = bank[7][:, T:2 * T]
                    pe.matmul(o, sv_stage[:, 0], aT_sb[:, 0:T], start=True, stop=False)
                    pe.matmul(o[:, P:T], sv_stage[:, 1], aT_sb[:, 2 * P:3 * P],
                              start=False, stop=True).then_inc(sb_out, 1)
                    for t in range(TT):
                        mm = pe.transpose(bank[6][:, t * P:(t + 1) * P], diff[:, t * P:(t + 1) * P], ident[:])
                    mm.then_inc(head_turned, 1)

            with pe.Fori(0, GATE_BLOCKS // PAIR) as i:
                for j in range(PAIR):
                    head = i * PAIR + j
                    pe.wait_ge(staged, head + 1)
                    for n in range(4):
                        for t in range(TT):
                            c = (n % 2) * T + t * P
                            mm = pe.transpose(bank[4 + n // 2][:, c:c + P], stage[:, t, n], ident[:])
                    mm.then_inc(qk_turned, 1)
                    project(head + IN_BLOCKS, j, i + TURN_GATE, lambda q: attend(head, q))

            def turn_mixed(n):
                pe.wait_ge(mixed, 2 * n + 2)
                for c in range(2):
                    if n:
                        pe.wait_ge(mixT_made, 2 * n + c - 1)
                    for k in range(2):
                        for t in range(TT):
                            at = (2 * c + k) * P
                            mm = pe.transpose(bank[6 + c][:, k * T + t * P:k * T + (t + 1) * P],
                                              gate_cols[:, t, n, at:at + P], ident[:])
                    mm.then_inc(mix_turned, 1)

            for n in range(2 * OUT_BLOCKS):
                pair = 2 * (n % 3)
                if n < 2:
                    pe.wait_ge(proj_act, 1 + IN_BLOCKS + GATE_BLOCKS + n)
                    pe.wait_ge(proj_dve, 1 + IN_BLOCKS + GATE_BLOCKS + n)
                if n >= 3:
                    pe.wait_ge(mixed, n - 2)
                wait_dense(n % RING, TURN_BR + n // RING)
                for k in range(KH):
                    if n < 2 and k == KH - 1:
                        pe.wait_ge((sbT_dve, diffT_act)[n % 2], 1 + HEADS)
                    for t in range(TT):
                        mm = pe.matmul(bank[pair + t][:], (sbT, diffT)[n % 2][:, k, t],
                                       slot(n % RING)[:, k], start=(k == 0), stop=(k == KH - 1))
                mm.then_inc(slots_used, 1)
                if n % 2 and n > 1:
                    turn_mixed(n // 2 - 1)
            for n in range(OUT_BLOCKS):
                pair = 2 * (n % 2)
                if n >= 2:
                    pe.wait_ge(x_added, TT * (n - 1))
                for half in range(2):
                    m = 2 * n + half
                    if n == 0 and half == 0:
                        pe.wait_ge(mixed, 2 * OUT_BLOCKS - 1)
                        pe.wait_ge(mixT_made, OUT_BLOCKS)
                    wait_dense(m % RING, TURN_OUT + m // RING)
                    for k in range(KH):
                        for t in range(TT):
                            mm = pe.matmul(bank[pair + t][:], mixT[:, KH * half + k, t * P:(t + 1) * P],
                                           slot(m % RING)[:, k], start=(half == 0 and k == 0),
                                           stop=(half == 1 and k == KH - 1))
                    mm.then_inc(slots_used, 1)
                    if n == 0 and half == 0:
                        turn_mixed(OUT_BLOCKS - 1)
                        pe.wait_ge(mixT_made, 2 * OUT_BLOCKS)
                    if n and half == 0:
                        turn_x2(n - 1)
                    if n == 1 and half == 0:
                        pe.wait_ge(route_in, 16 * 5)
                    if 0 < n < OUT_BLOCKS - 1 and half == 1:
                        route_block(n - 1)
            route_block(OUT_BLOCKS - 2)
            turn_x2(OUT_BLOCKS - 1)
            route_block(OUT_BLOCKS - 1).then_inc(logits_made, 1)
            pe.wait_ge(chosen_made, 1)
            for t in range(TT):
                for u in range(t + 1):
                    pe.matmul(bank[1][:, t * NE:(t + 1) * NE], (before_b if u == t else ones_b)[:],
                              chosen_b[:, u], start=(u == 0), stop=(u == t))
            for u in range(TT):
                mm = pe.matmul(bank[1][:, TT * NE:(TT + 1) * NE], ones_b[:], chosen_b[:, u],
                               start=(u == 0), stop=(u == TT - 1))
            mm.then_inc(ranks_made, 1)

            def experts(m):
                def wait_half(n, q):
                    s = (n + RING) % MOE_RING
                    turns = m * MOE_TURNS + (n // MOE_RING + 1 + (TURN_MOE if s < RING else 0))
                    pe.wait_ge(slot_full[s][q], turns * 16)
                    return slot(s)[:, 4 * q:4 * q + 4]

                def combine_block(b):
                    pe.wait_ge((y_dve, y_act)[b % 2], m * (OUT_BLOCKS // 2) + b // 2 + 1)
                    for t in range(TT):
                        n = TT * b + t
                        if n >= 4:
                            pe.wait_ge(added, m * (4 * TT) + (n - 2))
                        pe.matmul(bank[(2 + n) % 4][:], placeT[:, t * P:(t + 1) * P],
                                  y_sb[:, b * BLK:(b + 1) * BLK], start=True, stop=True).then_inc(combined, 1)

                def gather(q):
                    if q % 2 == 0:
                        pe.wait_ge(normed_made, TT * (q // 2 + 1))
                    if q >= 2:
                        pe.wait_ge(xg_made, m * KH + q - 1)
                    for k in range(2):
                        for t in range(TT):
                            mm = pe.matmul(bank[2 + q % 2][:, k * P:(k + 1) * P],
                                           normed[:, t, (2 * q + k) * P:(2 * q + k + 1) * P],
                                           pick[:, 0, t], start=(t == 0), stop=(t == TT - 1))
                    mm.then_inc(gathered, 1)

                pe.wait_ge(picks_made, m + 1)
                pe.wait_ge(added, m * 2 * TT * 2 + 1)
                gather(0)
                for k in range(KD):
                    if k % 2 and k < KD - 1:
                        gather(k // 2 + 1)
                    if k == 12:
                        pe.wait_ge(places_made, m + 1)
                        for t in range(TT):
                            mm = pe.transpose(bank[5][:, t * P:(t + 1) * P], pick[:, 1, t], ident[:])
                        mm.then_inc(place_turned, 1)
                    if k % 2 == 0:
                        pe.wait_ge(xg_made, m * KH + k // 2 + 1)
                    for w in (1, 0):
                        weights = wait_half(k, w)
                        for j in range(SIDE):
                            c = slice(j * SLOTS, (j + 1) * SLOTS)
                            mm = pe.matmul(bank[w][c, :], xgT[:, k, c], weights[:, j],
                                           start=(k == 0), stop=(k == KD - 1),
                                           tile_position=(0, j * SLOTS))
                    mm.then_inc(slots_used, 1)
                pe.wait_ge(act_made, m + 1)
                for f in range(FF // P):
                    mm = pe.transpose(bank[4][:, f * P:(f + 1) * P], act_sb[:, 1, f * P:(f + 1) * P], ident[:])
                mm.then_inc(act_turned, 1)
                pe.wait_ge(actT_made, m + 1)
                pe.wait_ge(placeT_made, m + 1)
                for n in range(2 * OUT_BLOCKS):
                    b = n // 2
                    for u in (1, 0):
                        weights = wait_half(KD + n, u)
                        f = 2 * (n % 2) + u
                        for j in range(SIDE):
                            c = slice(j * SLOTS, (j + 1) * SLOTS)
                            mm = pe.matmul(bank[4 + b][c, :], actT[:, f, c], weights[:, j],
                                           start=(f == 1), stop=(f == FF // P - 2),
                                           tile_position=(0, j * SLOTS))
                    mm.then_inc(slots_used, 1)
                    if b and n % 2 == 0:
                        combine_block(b - 1)
                combine_block(OUT_BLOCKS - 1)

            with pe.Fori(0, GROUPS) as g:
                experts(g)
            pe.wait_ge(passes_made, 1)
            passes = pe.value_load(passes_i[0:1, 0:1], min_val=1, max_val=MAX_PASSES)
            with pe.If(passes > 1):
                with pe.Fori(1, passes) as again:
                    with pe.Fori(0, GROUPS) as g:
                        experts(again * GROUPS + g)

        @block.scalar
        def _(act):
            act.sem_inc(proj_act, 2)
            act.sem_inc(diffT_act, 1)
            with nc.allow_non_contiguous_dma("small vectors"):
                act.dma_start(g_mix_sb[:], vec(g_mix)).then_inc(g_mix_in, 16)

            for t in range(TT):
                act.wait_ge(x_in[t], 16)
                if t:
                    with nc.allow_non_contiguous_dma("small vectors"):
                        act.dma_start(lam_sb[:], lambda_params[0].partition_broadcast(P)).then_inc(early_in, 16)
                        act.dma_start(gsub[:], g_subln[0].partition_broadcast(P)).then_inc(early_in, 16)
                        act.dma_start(pos_i[:], positions.rearrange("a (t p) -> p (a t)", p=P)).then_inc(early_in, 16)
                    act.drain()
                act.activation(junk, x_tok[:, t], ACT.Square, accum_out=ssq[:, t, 0:1])
            act.drain().then_inc(squared, 1)
            act.wait_ge(lam_summed, 1)
            act.activation(lam_two[:], lam_two[:], ACT.Exp).then_inc(lam_exped, 1)
            act.wait_ge(angles_made, 1)
            act.activation(sin[:], angle[:], ACT.Sin).then_inc(sines_made, 1)
            act.activation(cos[:], angle[:], ACT.Sin, scale=0.5).then_inc(angles_made, 1)

            def copy_block(n, j, dst):
                act.wait_ge(slots_used, (n + 1) * 2 + RING)
                act.activation(dst, bank[2 * j][:], ACT.Copy, scale=rstd_in[:, 0:1]).then_inc(proj_act, 1)

            act.wait_ge(rstd_made, 1)
            with act.Fori(0, TURN_GATE) as i:
                for j in range(PAIR):
                    dst = qkv_cols[:, 0].rearrange("p (i j) n -> p i j n", j=PAIR)[:, i, j]
                    copy_block(i * PAIR + j, j, dst)

            with act.Fori(0, GATE_BLOCKS // PAIR) as i:
                for j in range(PAIR):
                    head = i * PAIR + j
                    act.wait_ge(qk_turned, head + 2)
                    act.activation(qkT[:, 0:2], bank[4][:], ACT.Copy).then_inc(qkT_act, 1)
                    act.wait_ge(tops_made, head + 1)
                    for t in range(TT):
                        for m in range(2):
                            p_ = prob[:, m, 0:P] if t == 0 else prob[:, m, P:3 * P]
                            act.activation(p_, p_, ACT.Exp, bias=neg_top[:, t, m:m + 1],
                                           accum_out=total[:, t, m:m + 1])
                    act.drain().then_inc(diff_exped, 1)
                    act.wait_ge(z_made, head + 1)
                    act.activation(soft[:], z[:], ACT.Abs)
                    act.drain()
                    act.activation(soft[:], soft[:], ACT.Exp, scale=-1.0)
                    act.drain()
                    act.activation(soft[:], soft[:], ACT.Ln, bias=1.0).then_inc(soft_made, 1)
                    act.wait_ge(diff_turned, head + 1)
                    act.activation(aT_diff[:], bank[5][:, 0:3 * P], ACT.Copy).then_inc(aT_act, 1)
                    act.wait_ge(stick_summed, head + 1)
                    act.activation(stick[:], stick[:], ACT.Exp).then_inc(stick_exped, 1)
                    act.wait_ge(diff_out, head + 1)
                    for t in range(TT):
                        act.activation(soft[:, t * P:(t + 1) * P], bank[7][:, t * P:(t + 1) * P],
                                       ACT.Square, accum_out=ssq[:, t, 0:1])
                    act.drain().then_inc(head_squared, 1)
                    copy_block(head + IN_BLOCKS, j,
                               gate_cols[:, 0].rearrange("p (i j) n -> p i j n", j=PAIR)[:, i, j])
                    act.wait_ge(head_turned, head + 1)
                    act.activation(diffT[:, head], bank[6][:, 0:T].rearrange("p (t s) -> p t s", t=TT),
                                   ACT.Copy).then_inc(diffT_act, 1)

            act.wait_ge(proj_dve, 2 + IN_BLOCKS + GATE_BLOCKS)
            act.drain()
            for t in range(TT):
                act.activation(gates[:, t], gates[:, t], ACT.Sigmoid)
            act.drain().then_inc(gates_open, 1)
            for n in range(2 * OUT_BLOCKS):
                act.wait_ge(mix_turned, n + 1)
                act.activation(mixT[:, 2 * n:2 * n + 2].rearrange("p a b -> p (a b)"), bank[6 + n % 2][:],
                               ACT.Copy).then_inc(mixT_made, 1)
            act.wait_ge(route_in, 16 * 5)
            for n in range(OUT_BLOCKS):
                for t in range(TT):
                    act.wait_ge(x_added, TT * n + t + 1)
                    act.activation(squares, x_cols[:, t, n], ACT.Square, accum_out=ssq[:, t, n:n + 1])
                    act.drain()
                if n == OUT_BLOCKS - 1:
                    act.sem_inc(squared, 1)
                for c in range(2 if n == OUT_BLOCKS - 1 else 1):
                    act.wait_ge(turned, 2 * n + c + 1)
                    for k in range(2):
                        at = 4 * n + 2 * c + k
                        act.activation(x2T[:, at], bank[4 + c][:, k * T:(k + 1) * T], ACT.Copy,
                                       scale=g_moe_sb[:, at:at + 1]).then_inc(turned_act, 1)
            act.wait_ge(rstd_made, 2)
            act.wait_ge(logits_made, 1)
            for b in range(OUT_BLOCKS):
                if b == 2:
                    act.wait_ge(route_shifted, 1)
                    for t in range(TT):
                        act.activation(shifted[:, t, 0:NG], shifted[:, t, 0:NG], ACT.Exp,
                                       accum_out=pair_w[:, t, 0:1])
                    act.drain().then_inc(route_exped, 1)
                    act.wait_ge(route_shifted, 2)
                    act.activation(shifted[:, :, NG:NG + 1], shifted[:, :, NG:NG + 1],
                                   ACT.Exp).then_inc(route_exped, 1)
                for t in range(TT):
                    act.activation(normed[:, t, b * BLK:(b + 1) * BLK], x_cols[:, t, b], ACT.Copy,
                                   scale=rstd[:, t:t + 1]).then_inc(normed_made, 1)

            def experts(m):
                act.wait_ge(place_turned, m + 2)
                act.activation(placeT, bank[5][:, 0:T], ACT.Copy).then_inc(placeT_made, 1)
                act.wait_ge(slots_used, m * LOADS + (RING + USED_MOE + KD))
                act.activation(act_sb[:, 0], bank[0][:], ACT.Silu).then_inc(silu_made, 1)
                act.wait_ge(act_turned, m + 1)
                act.activation(actT.rearrange("p a b -> p (a b)"), bank[4][:], ACT.Copy).then_inc(actT_made, 1)
                for b in range(OUT_BLOCKS):
                    if b % 2:
                        act.wait_ge(slots_used, m * LOADS + (RING + USED_MOE + KD + 2 * (b + 1)))
                        act.activation(y_sb[:, b * BLK:(b + 1) * BLK], bank[4 + b][:], ACT.Copy).then_inc(y_act, 1)
                    for t in range(TT):
                        act.drain()
                        act.wait_ge(added, m * (4 * TT) + (TT * b + t + 2))
                        act.activation(squares, x_cols[:, t, b], ACT.Square, accum_out=ssq[:, t, b:b + 1])
                act.drain().then_inc(round_squared, 1)

            with act.Fori(0, GROUPS) as g:
                experts(g)
            act.wait_ge(passes_made, 1)
            passes = act.value_load(passes_i[0:1, 0:1], min_val=1, max_val=MAX_PASSES)
            with act.If(passes > 1):
                with act.Fori(1, passes) as again:
                    with act.Fori(0, GROUPS) as g:
                        experts(again * GROUPS + g)

        @block.vector
        def _(dve):
            dve.sem_inc(proj_dve, 2)
            dve.sem_inc(sbT_dve, 1)
            dve.sem_inc(added, 1)
            dve.sem_inc(place_turned, 1)

            def inverse_root(out_, sums, n):
                bits, guess = newton[:].bitcast(I32), out_.bitcast(I32)
                dve.tensor_scalar(var[:], sums, 1.0 / n, EPS, ALU.mult, ALU.add)
                dve.tensor_scalar(minus_half[:], sums, -0.5 / n, -0.5 * EPS, ALU.mult, ALU.add)
                dve.drain()
                dve.tensor_single_scalar(bits, var[:].bitcast(I32), 1, op=ALU.logical_shift_right)
                dve.drain()
                dve.tensor_scalar(guess, bits, -1.0, float(0x5f3759df), ALU.mult, ALU.add)
                for _ in range(3):
                    dve.drain()
                    for t in range(TT):
                        c = slice(t, t + 1)
                        dve.scalar_tensor_tensor(out=newton[:, c], in0=out_[:, c], scalar=out_[:, c],
                                                 in1=minus_half[:, c], op0=ALU.mult, op1=ALU.mult)
                    dve.drain()
                    dve.scalar_tensor_tensor(out=out_, in0=newton[:], scalar=1.5, in1=out_,
                                             op0=ALU.add, op1=ALU.mult)
                dve.drain()

            def norm(parts, out_):
                if parts > 1:
                    dve.tensor_reduce(sums[:], ssq[:, :, 0:parts], AX, ALU.add)
                    dve.drain()
                inverse_root(out_, sums[:] if parts > 1 else ssq[:, :, 0], D)

            dve.wait_ge(g_mix_in, 16)
            for n in range(4 * TT):
                t, m = n // 4, n % 4
                dve.wait_ge(x_turned, n + 1)
                dve.tensor_tensor(hT[:, 4 * m:4 * m + 4, t * P:(t + 1) * P],
                                  bank[n][:].rearrange("p (k s) -> p k s", k=4),
                                  g_mix_sb[:, 4 * m:4 * m + 4].unsqueeze(2).broadcast_to([P, 4, P]),
                                  ALU.mult).then_inc(xT_made, 1)
            dve.wait_ge(squared, 1)
            norm(1, rstd_in[:])
            dve.sem_inc(rstd_made, 1)
            dve.wait_ge(early_in, 16 * 3)
            lam_prod = stick[:, 0:2 * HQ].rearrange("p (a b) -> p a b", a=2)
            lam_v = lam_sb[:, :, :].rearrange("p (a b) d -> p a b d", b=2)
            dve.tensor_tensor(lam_prod, lam_v[:, :, 0], lam_v[:, :, 1], ALU.mult)
            dve.drain()
            dve.tensor_reduce(lam_two[:], lam_prod, AX, ALU.add).then_inc(lam_summed, 1)
            dve.wait_ge(lam_exped, 1)
            dve.tensor_scalar(neg_lam[:], lam_two[:, 0:1], -1.0, -LAMBDA_INIT, ALU.mult, ALU.add)
            dve.drain()
            dve.tensor_tensor(neg_lam[:], neg_lam[:], lam_two[:, 1:2], ALU.add)
            dve.tensor_scalar(gsub[:], gsub[:], 1.0 - LAMBDA_INIT, None, ALU.mult)
            dve.wait_ge(masks_made, 1)
            dve.tensor_copy(pos_f[:], pos_i[:])
            dve.drain()
            for t in range(TT):
                dve.tensor_scalar(angle[:, t], inv_freq[:], pos_f[:, t:t + 1], None, ALU.mult)
            dve.drain()
            dve.tensor_scalar(whole[:], angle[:], float(1 / (2 * np.pi)), None, ALU.mult)
            dve.drain()
            dve.tensor_scalar(whole[:], whole[:], ROUND, None, ALU.add)
            dve.drain()
            dve.tensor_scalar(whole[:], whole[:], -ROUND, None, ALU.add)
            for c in TWO_PI:
                dve.drain()
                dve.scalar_tensor_tensor(out=angle[:], in0=whole[:], scalar=-c, in1=angle[:],
                                         op0=ALU.mult, op1=ALU.add)
            dve.drain()
            dve.tensor_scalar(angle[:], angle[:], 3.1415925, -3.1415925, ALU.min, ALU.max).then_inc(angles_made, 1)
            dve.wait_ge(angles_made, 2)
            dve.tensor_tensor(cos[:], cos[:], cos[:], ALU.mult)
            dve.drain()
            dve.tensor_scalar(cos[:], cos[:], -2.0, 1.0, ALU.mult, ALU.add)
            dve.drain()
            dve.wait_ge(sines_made, 1)
            dve.sem_inc(sines_made, 1)

            def copy_block(n, j, dst):
                dve.wait_ge(slots_used, (n + 1) * 2 + RING)
                dve.tensor_scalar(dst, bank[2 * j + 1][:], rstd_in[:, 1:2], None, ALU.mult).then_inc(proj_dve, 1)

            with dve.Fori(0, TURN_GATE) as i:
                for j in range(PAIR):
                    copy_block(i * PAIR + j, j, qkv_cols[:, 1].rearrange("p (i j) n -> p i j n", j=PAIR)[:, i, j])

            with dve.Fori(0, GATE_BLOCKS // PAIR) as i:
                for j in range(PAIR):
                    head = i * PAIR + j
                    dve.wait_ge(qk_turned, head + 2)
                    dve.tensor_copy(qkT[:, 2:4].rearrange("p a b -> p (a b)"), bank[5][:]).then_inc(qkT_dve, 1)
                    dve.wait_ge(diff_scored, head + 1)
                    for m in range(2):
                        dve.scalar_tensor_tensor(out=prob[:, m], in0=bank[6 + m][:, 0:3 * P], scalar=HQ ** -0.5,
                                                 in1=mask_upto[:], op0=ALU.mult, op1=ALU.add)
                    dve.drain()
                    dve.tensor_reduce(top[:, 0], prob[:, :, 0:P], AX, ALU.max)
                    dve.tensor_reduce(top[:, 1], prob[:, :, P:3 * P], AX, ALU.max)
                    dve.drain()
                    dve.tensor_scalar(neg_top[:], top[:], -1.0, None, ALU.mult).then_inc(tops_made, 1)
                    dve.wait_ge(sb_scored, head + 1)
                    dve.scalar_tensor_tensor(out=z[:], in0=bank[4][:, 0:3 * P], scalar=P ** -0.5,
                                             in1=mask_before[:], op0=ALU.mult, op1=ALU.add).then_inc(z_made, 1)
                    dve.wait_ge(diff_exped, head + 1)
                    dve.reciprocal(weight[:], total[:])
                    dve.drain()
                    dve.tensor_scalar(weight[:, :, 1], weight[:, :, 1], neg_lam[:], None, ALU.mult)
                    for t in range(TT):
                        c = slice(0, P) if t == 0 else slice(P, 3 * P)
                        dve.tensor_scalar(diff[:, c], prob[:, 0, c], weight[:, t, 0:1], None, ALU.mult)
                    dve.drain()
                    for t in range(TT):
                        c = slice(0, P) if t == 0 else slice(P, 3 * P)
                        dve.scalar_tensor_tensor(out=diff[:, c], in0=prob[:, 1, c], scalar=weight[:, t, 1:2],
                                                 in1=diff[:, c], op0=ALU.mult, op1=ALU.add)
                    dve.drain().then_inc(diff_made, 1)
                    dve.wait_ge(soft_made, head + 1)
                    dve.scalar_tensor_tensor(out=soft[:], in0=z[:], scalar=0.0, in1=soft[:],
                                             op0=ALU.max, op1=ALU.add)
                    dve.drain()
                    for c in (slice(0, P), slice(P, 3 * P)):
                        dve.tensor_tensor_scan(stick[:, c][:, ::-1], soft[:, c][:, ::-1], soft[:, c][:, ::-1],
                                               0.0, ALU.add, ALU.max)
                    dve.drain()
                    dve.tensor_tensor(stick[:], z[:], stick[:], ALU.subtract).then_inc(stick_summed, 1)
                    dve.wait_ge(sb_turned, head + 1)
                    dve.tensor_copy(aT_sb[:], bank[6][:, 0:3 * P]).then_inc(aT_dve, 1)
                    dve.wait_ge(head_squared, head + 1)
                    inverse_root(rstd[:], ssq[:, :, 0], HV)
                    for t in range(TT):
                        dve.scalar_tensor_tensor(out=diff[:, t * P:(t + 1) * P], in0=bank[7][:, t * P:(t + 1) * P],
                                                 scalar=rstd[:, t:t + 1], in1=gsub[:], op0=ALU.mult, op1=ALU.mult)
                    dve.drain().then_inc(head_normed, 1)
                    copy_block(head + IN_BLOCKS, j,
                               gate_cols[:, 1].rearrange("p (i j) n -> p i j n", j=PAIR)[:, i, j])
                    dve.wait_ge(sb_out, head + 2)
                    dve.tensor_copy(sbT[:, head], bank[7][:, T:2 * T].rearrange("p (t s) -> p t s", t=TT)
                                    ).then_inc(sbT_dve, 1)

            dve.wait_ge(gates_open, 1)
            for n in range(2 * OUT_BLOCKS):
                pair = 2 * (n % 3)
                dve.wait_ge(slots_used, RING * (TURN_BR + 1) + n + 1)
                for t in range(TT):
                    g = gate_cols[:, t, (1 - n % 2) * OUT_BLOCKS + n // 2]
                    dve.tensor_tensor(g, g, bank[pair + t][:], ALU.mult)
                dve.drain()
                if n % 2 == 0:
                    dve.sem_inc(mixed, 1)
                else:
                    for t in range(TT):
                        g0, g1 = gate_cols[:, t, n // 2], gate_cols[:, t, OUT_BLOCKS + n // 2]
                        dve.tensor_tensor(g0, g0, g1, ALU.add)
                    dve.drain().then_inc(mixed, 1)
            for n in range(OUT_BLOCKS):
                pair = 2 * (n % 2)
                dve.wait_ge(slots_used, RING * (TURN_OUT + 1) + 2 * n + 2)
                for t in range(TT):
                    dve.tensor_tensor(x_cols[:, t, n], x_cols[:, t, n], bank[pair + t][:], ALU.add).then_inc(x_added, 1)
                if n == 0:
                    dve.wait_ge(route_in, 16 * 5)
                if n == OUT_BLOCKS - 1:
                    break
                dve.wait_ge(turned, 2 * n + 2)
                for k in range(2):
                    dve.tensor_scalar(x2T[:, 4 * n + 2 + k], bank[5][:, k * T:(k + 1) * T],
                                      g_moe_sb[:, 4 * n + 2 + k:4 * n + 3 + k], None, ALU.mult).then_inc(turned_dve, 1)
            dve.wait_ge(squared, 2)
            norm(OUT_BLOCKS, rstd[:])
            dve.sem_inc(rstd_made, 1)

            def bc(v, n):
                return v.broadcast_to([P, TT, n])

            def not_first_max(out_, values, top_, n):
                dve.tensor_tensor(out_, values, bc(top_, n), ALU.is_equal)
                dve.drain()
                fall = falling[:].unsqueeze(1).broadcast_to([P, TT, n])
                dve.tensor_tensor(tie[:, :, 0:n], out_, fall, ALU.mult)
                dve.drain()
                dve.tensor_reduce(tie_top, tie[:, :, 0:n], AX, ALU.max)
                dve.drain()
                dve.tensor_tensor(out_, tie[:, :, 0:n], bc(tie_top, n), ALU.not_equal)
                dve.drain()

            dve.wait_ge(logits_made, 1)
            for t in range(TT):
                dve.scalar_tensor_tensor(out=logits[:, t], in0=bank[6 + t][:, 0:NG + NE], scalar=rstd[:, t:t + 1],
                                         in1=b_route[:], op0=ALU.mult, op1=ALU.add)
            dve.drain()
            dve.tensor_reduce(best[:, :, 0:1], logits[:, :, 0:NG], AX, ALU.max)
            dve.drain()
            not_first_max(is_other, logits[:, :, 0:NG], best[:, :, 0:1], NG)
            dve.tensor_tensor(shifted[:, :, 0:NG], logits[:, :, 0:NG], bc(best[:, :, 0:1], NG),
                              ALU.subtract).then_inc(route_shifted, 1)
            for t in range(TT):
                dve.scalar_tensor_tensor(out=masked[:, t].rearrange("p (g e) -> p g e", g=NG),
                                         in0=is_other[:, t].unsqueeze(2).broadcast_to([P, NG, PER]), scalar=-BIG,
                                         in1=logits[:, t, NG:].rearrange("p (g e) -> p g e", g=NG),
                                         op0=ALU.mult, op1=ALU.add)
            dve.drain()
            for t in range(TT):
                dve.max(best8[:, t], masked[:, t])
            dve.drain()
            for t in range(TT):
                dve.max_index(place8[:, t], best8[:, t], masked[:, t])
            dve.drain()
            dve.tensor_copy(best_at, place8[:, :, 0:2])
            dve.drain()
            for c in range(2):
                dve.tensor_tensor(is_top[c], expert_id[:].unsqueeze(1).broadcast_to([P, TT, NE]),
                                  bc(best_at[:, :, c:c + 1], NE), ALU.is_equal)
            dve.drain()
            dve.tensor_tensor(chosen_b[:], is_top[0], is_top[1], ALU.add).then_inc(chosen_made, 1)
            dve.tensor_tensor(shifted[:, :, NG:NG + 1], best8[:, :, 1:2], best8[:, :, 0:1],
                              ALU.subtract).then_inc(route_shifted, 1)
            dve.tensor_tensor(chosen, is_top[0], is_top[1], ALU.add)
            dve.drain()
            dve.wait_ge(route_exped, 2)
            dve.scalar_tensor_tensor(out=pair_w[:, :, 1:2], in0=shifted[:, :, NG:NG + 1], scalar=1.0,
                                     in1=pair_w[:, :, 0:1], op0=ALU.add, op1=ALU.mult)
            dve.drain()
            dve.reciprocal(pair_w[:, :, 2:3], pair_w[:, :, 1:2])
            dve.drain().then_inc(first_weighed, 1)
            dve.wait_ge(ranks_made, 1)
            dve.scalar_tensor_tensor(out=rank, in0=bank[1][:, 0:TT * NE].rearrange("p (t n) -> p t n", t=TT),
                                     scalar=float(2 * T), in1=chosen, op0=ALU.add, op1=ALU.mult)
            dve.tensor_reduce(count[:, 0:1], bank[1][:, TT * NE:(TT + 1) * NE], AX, ALU.max)
            dve.drain().then_inc(count_made, 1)
            dve.tensor_scalar(rank, rank, -float(2 * T), None, ALU.add)
            dve.drain()

            def experts(m, g):
                dve.drain()
                dve.wait_ge(place_turned, m + 1)
                def by_expert(v, t):
                    return (v[:, t].rearrange("p (g e) -> p g e", e=SIDE)[:, g]
                            .unsqueeze(2).broadcast_to([P, SIDE, SLOTS]))

                def by_slot(n, t):
                    return pick[:, n, t].rearrange("p (e s) -> p e s", e=SIDE)

                for t in range(TT):
                    dve.tensor_tensor(by_slot(0, t), slot_id[:].unsqueeze(1).broadcast_to([P, SIDE, SLOTS]),
                                      by_expert(rank, t), ALU.is_equal)
                dve.drain().then_inc(picks_made, 1)
                dve.wait_ge(combine_made, 1)
                for t in range(TT):
                    dve.tensor_tensor(by_slot(1, t), by_slot(0, t), by_expert(combine, t), ALU.mult)
                dve.drain().then_inc(places_made, 1)
                for q in range(KH):
                    dve.wait_ge(gathered, m * KH + q + 1)
                    dve.tensor_tensor(xgT[:, 2 * q:2 * q + 2],
                                      bank[2 + q % 2][:, 0:2 * P].rearrange("p (k s) -> p k s", k=2),
                                      g_moe_sb[:, 2 * q:2 * q + 2].unsqueeze(2).broadcast_to([P, 2, P]),
                                      ALU.mult).then_inc(xg_made, 1)
                dve.wait_ge(silu_made, m + 1)
                dve.tensor_tensor(act_sb[:, 1], act_sb[:, 0], bank[1][:], ALU.mult).then_inc(act_made, 1)
                for b in range(OUT_BLOCKS):
                    if b % 2 == 0:
                        dve.wait_ge(slots_used, m * LOADS + (RING + USED_MOE + KD + 2 * (b + 1)))
                        dve.tensor_copy(y_sb[:, b * BLK:(b + 1) * BLK], bank[4 + b][:]).then_inc(y_dve, 1)
                    for t in range(TT):
                        dve.wait_ge(combined, m * (4 * TT) + (TT * b + t + 1))
                        dve.tensor_tensor(x_cols[:, t, b], x_cols[:, t, b], bank[(2 + TT * b + t) % 4][:],
                                          ALU.add).then_inc(added, 1)

            with dve.Fori(0, GROUPS) as g:
                experts(g, g)
            dve.wait_ge(passes_made, 1)
            passes = dve.value_load(passes_i[0:1, 0:1], min_val=1, max_val=MAX_PASSES)
            with dve.If(passes > 1):
                dve.drain()
                dve.tensor_scalar(rank, rank, -float(SLOTS), None, ALU.add)
                with dve.Fori(1, passes) as again:
                    with dve.Fori(0, GROUPS) as g:
                        experts(again * GROUPS + g, g)
                    dve.drain()
                    dve.wait_ge(round_squared, again * GROUPS + GROUPS)
                    dve.tensor_scalar(rank, rank, -float(SLOTS), None, ALU.add)
            dve.drain()
            dve.wait_ge(round_squared, GROUPS)
            norm(OUT_BLOCKS, rstd[:])
            dve.wait_ge(g_final_in, 16)
            for t, c in [(t, slice(c, c + BLK)) for t in range(TT) for c in range(0, D, BLK)]:
                dve.scalar_tensor_tensor(out=normed[:, t, c], in0=x_tok[:, t, c], scalar=rstd[:, t:t + 1],
                                         in1=g_final_sb[:, c], op0=ALU.mult, op1=ALU.mult).then_inc(out_made, 1)


_INS = ["x", "positions", "g_mix", "w_in", "w_gate", "lambda_params", "g_subln", "w_br_diff",
        "w_br_sb", "w_out", "g_moe", "w_group", "b_group", "w_router", "b_router", "w_up_gate",
        "w_up", "w_down", "g_final"]


def kernel(**inputs):
    import numpy as _np
    import concourse.bacc as _bacc
    from concourse import mybir as _mybir
    from concourse.bass_utils import run_bass_kernel_spmd as _run

    nc = _bacc.Bacc("TRN2", target_bir_lowering=False, num_devices=1)
    arrays, args = {}, []
    for name in _INS:
        a = _np.ascontiguousarray(inputs[name])
        arrays[f"in_{name}"] = a
        args.append(nc.dram_tensor(f"in_{name}", a.shape, _mybir.dt.from_np(a.dtype), kind="ExternalInput").ap())
    out = nc.dram_tensor("block_out", inputs["x"].shape, _mybir.dt.float32, kind="ExternalOutput").ap()
    decoder_block(nc, *args, out)
    r = _run(nc, [arrays], core_ids=[0])
    return r.results[0]["block_out"]
```
